# Optimizing a Trainium2 kernel written in Bass

```python
import jax, jax.numpy as jnp
from jax import lax
import numpy as np
import math
import jax
import jax.numpy as jnp

D_MODEL = 1024
BATCH = 1
SEQ = 512
DEPTH = 2

PLE_DIM = 256
N_EVEN = (DEPTH + 1) // 2
N_ODD = DEPTH // 2
RG_WIDTH = 512
RG_BLOCKS = 8
RG_BLOCK = RG_WIDTH // RG_BLOCKS
RG_CONV = 4
RG_C = 8.0
ML_HEADS = 4
ML_HEAD_DIM = 128
ML_WIDTH = ML_HEADS * ML_HEAD_DIM
ML_CONV = 4
ML_CHUNK = 64
HY_IN = 2 * RG_WIDTH + 4 * ML_WIDTH + 2 * ML_HEADS
HY_MIX = RG_WIDTH + ML_WIDTH
AT_HEADS = 16
AT_KV_HEADS = 4
AT_HEAD_DIM = 64
WINDOW = 128
ROPE_THETA = 10000.0
AT_QKV = (AT_HEADS + 2 * AT_KV_HEADS) * AT_HEAD_DIM
FF_DIM = 3 * D_MODEL
FF_CONV = 3
EPS = 1e-6


def rms_norm(x, g):
    xf = x.astype(jnp.float32)
    y = xf * lax.rsqrt(jnp.mean(xf * xf, axis=-1, keepdims=True) + EPS)
    return (y * g.astype(jnp.float32)).astype(x.dtype)

def causal_dwconv(x, w, b):
    k_w = w.shape[0]
    s = x.shape[1]
    xp = jnp.pad(x, ((0, 0), (k_w - 1, 0), (0, 0)))
    y = xp[:, 0:s] * w[0]
    for j in range(1, k_w):
        y = y + xp[:, j:j + s] * w[j]
    return y + b

def _linear_recurrence_combine(left, right):
    a_l, b_l = left
    a_r, b_r = right
    return a_l * a_r, a_r * b_l + b_r

def rg_lru(x, w_a, b_a, w_x, b_x, lam):
    f32 = jnp.float32
    bsz, s, _ = x.shape
    xf = x.astype(f32)
    xb = xf.reshape(bsz, s, RG_BLOCKS, RG_BLOCK)
    r = jax.nn.sigmoid(jnp.einsum('bsni,nij->bsnj', xb, w_a.astype(f32)).reshape(bsz, s, RG_WIDTH) + b_a.astype(f32))
    i = jax.nn.sigmoid(jnp.einsum('bsni,nij->bsnj', xb, w_x.astype(f32)).reshape(bsz, s, RG_WIDTH) + b_x.astype(f32))
    log_a = -RG_C * r * jax.nn.softplus(-lam.astype(f32))
    a = jnp.exp(log_a)
    u = jnp.sqrt(-jnp.expm1(2.0 * log_a)) * (i * xf)
    _, h = lax.associative_scan(_linear_recurrence_combine, (a, u), axis=1)
    return h

def mlstm_chunkwise(q, k, v, i_pre, f_pre):
    f32 = jnp.float32
    bsz, s, nh, dh = q.shape
    nc = s // ML_CHUNK

    def to_chunks(t):
        return t.astype(f32).reshape(bsz, nc, ML_CHUNK, nh, dh).transpose(0, 3, 1, 2, 4)

    def gate_chunks(t):
        return t.astype(f32).reshape(bsz, nc, ML_CHUNK, nh).transpose(0, 3, 1, 2)

    qc = to_chunks(q)
    kc = to_chunks(k) * (dh ** -0.5)
    vc = to_chunks(v)
    log_i = gate_chunks(i_pre)
    log_f = jax.nn.log_sigmoid(gate_chunks(f_pre))
    b = jnp.cumsum(log_f, axis=-1)
    b_last = b[..., -1]

    g = b_last[..., None] - b + log_i
    m_loc = jnp.max(g, axis=-1)
    w_loc = jnp.exp(g - m_loc[..., None])
    c_loc = jnp.einsum('bhcl,bhcld,bhcle->bhcde', w_loc, kc, vc)
    n_loc = jnp.einsum('bhcl,bhcld->bhcd', w_loc, kc)

    def step(carry, inp):
        c_st, n_st, m_st = carry
        c_l, n_l, m_l, b_l = inp
        m_new = jnp.maximum(b_l + m_st, m_l)
        a_prev = jnp.exp(b_l + m_st - m_new)
        a_loc = jnp.exp(m_l - m_new)
        c_new = a_prev[..., None, None] * c_st + a_loc[..., None, None] * c_l
        n_new = a_prev[..., None] * n_st + a_loc[..., None] * n_l
        return (c_new, n_new, m_new), (c_st, n_st, m_st)

    init = (jnp.zeros((bsz, nh, dh, dh), f32), jnp.zeros((bsz, nh, dh), f32), jnp.full((bsz, nh), -jnp.inf, f32))
    xs = (jnp.moveaxis(c_loc, 2, 0), jnp.moveaxis(n_loc, 2, 0), jnp.moveaxis(m_loc, 2, 0), jnp.moveaxis(b_last, 2, 0))
    _, (c_prev, n_prev, m_prev) = lax.scan(step, init, xs)
    c_prev = jnp.moveaxis(c_prev, 0, 2)
    n_prev = jnp.moveaxis(n_prev, 0, 2)
    m_prev = jnp.moveaxis(m_prev, 0, 2)

    idx = jnp.arange(ML_CHUNK)
    causal = idx[:, None] >= idx[None, :]
    d_log = b[..., :, None] - b[..., None, :] + log_i[..., None, :]
    d_log = jnp.where(causal, d_log, -jnp.inf)
    inter_log = b + m_prev[..., None]
    m_t = jnp.maximum(inter_log, jnp.max(d_log, axis=-1))
    w_intra = jnp.exp(d_log - m_t[..., None])
    a_inter = jnp.exp(inter_log - m_t)
    s_qk = jnp.einsum('bhctd,bhcsd->bhcts', qc, kc) * w_intra
    num = jnp.einsum('bhcts,bhcse->bhcte', s_qk, vc) + a_inter[..., None] * jnp.einsum('bhctd,bhcde->bhcte', qc, c_prev)
    den = jnp.sum(s_qk, axis=-1) + a_inter * jnp.einsum('bhctd,bhcd->bhct', qc, n_prev)
    h = num / jnp.maximum(jnp.abs(den), jnp.exp(-m_t))[..., None]
    return h.transpose(0, 2, 3, 1, 4).reshape(bsz, s, nh, dh)

def rglru_mlstm_mixer(h, w_in, b_in, rg_conv_w, rg_conv_b, rg_w_a, rg_b_a, rg_w_x, rg_b_x, rg_lambda,
                      ml_conv_w, ml_conv_b, ml_norm, w_out):
    f32 = jnp.float32
    bsz, s, _ = h.shape
    z = h @ w_in + b_in
    cuts = [RG_WIDTH, 2 * RG_WIDTH, 2 * RG_WIDTH + ML_WIDTH, 2 * RG_WIDTH + 2 * ML_WIDTH,
            2 * RG_WIDTH + 3 * ML_WIDTH, 2 * RG_WIDTH + 4 * ML_WIDTH, 2 * RG_WIDTH + 4 * ML_WIDTH + ML_HEADS]
    x_rg, g_rg, q, k, v, o, i_pre, f_pre = jnp.split(z, cuts, axis=-1)
    xc = causal_dwconv(x_rg, rg_conv_w, rg_conv_b)
    y_rg = rg_lru(xc, rg_w_a, rg_b_a, rg_w_x, rg_b_x, rg_lambda) * jax.nn.gelu(g_rg.astype(f32), approximate=True)
    qk = jax.nn.silu(causal_dwconv(jnp.concatenate([q, k], axis=-1), ml_conv_w, ml_conv_b))
    q, k = jnp.split(qk, 2, axis=-1)
    hm = mlstm_chunkwise(q.reshape(bsz, s, ML_HEADS, ML_HEAD_DIM), k.reshape(bsz, s, ML_HEADS, ML_HEAD_DIM),
                         v.reshape(bsz, s, ML_HEADS, ML_HEAD_DIM), i_pre, f_pre)
    hm = rms_norm(hm, ml_norm.reshape(ML_HEADS, ML_HEAD_DIM))
    y_ml = jax.nn.sigmoid(o.astype(f32)) * hm.reshape(bsz, s, ML_WIDTH)
    y = jnp.concatenate([y_rg, y_ml], axis=-1).astype(h.dtype)
    return y @ w_out

def rope_tables(positions):
    half = AT_HEAD_DIM // 2
    inv_freq = ROPE_THETA ** (-jnp.arange(half, dtype=jnp.float32) * (2.0 / AT_HEAD_DIM))
    ang = positions.astype(jnp.float32)[..., None] * inv_freq
    return jnp.cos(ang)[:, :, None, :], jnp.sin(ang)[:, :, None, :]

def apply_rope(x, cos, sin):
    xf = x.astype(jnp.float32)
    x1, x2 = jnp.split(xf, 2, axis=-1)
    return jnp.concatenate([x1 * cos - x2 * sin, x2 * cos + x1 * sin], axis=-1)

def banded_sink_attention(q, k, v, sinks):
    f32 = jnp.float32
    bsz, s, _, dh = q.shape
    nb = s // WINDOW
    grp = AT_HEADS // AT_KV_HEADS
    qb = q.astype(f32).reshape(bsz, nb, WINDOW, AT_KV_HEADS, grp, dh)

    def key_window(t):
        tb = t.astype(f32).reshape(bsz, nb, WINDOW, AT_KV_HEADS, dh)
        prev = jnp.pad(tb, ((0, 0), (1, 0), (0, 0), (0, 0), (0, 0)))[:, :-1]
        return jnp.concatenate([prev, tb], axis=2)

    kw = key_window(k)
    vw = key_window(v)
    logits = jnp.einsum('bnqhgd,bnkhd->bnhgqk', qb, kw) * (dh ** -0.5)
    qi = jnp.arange(WINDOW)[:, None]
    kj = jnp.arange(2 * WINDOW)[None, :]
    band = (kj > qi) & (kj <= qi + WINDOW)
    blk = jnp.arange(nb)[:, None, None]
    valid = band[None] & ((blk > 0) | (kj >= WINDOW)[None])
    logits = jnp.where(valid[None, :, None, None], logits, -jnp.inf)
    sink = sinks.astype(f32).reshape(AT_KV_HEADS, grp)[:, :, None]
    m = jnp.maximum(jnp.max(logits, axis=-1), sink)
    probs = jnp.exp(logits - m[..., None])
    denom = jnp.sum(probs, axis=-1) + jnp.exp(sink - m)
    out = jnp.einsum('bnhgqk,bnkhd->bnhgqd', probs, vw) / denom[..., None]
    return out.transpose(0, 1, 4, 2, 3, 5).reshape(bsz, s, AT_HEADS * dh)

def swa_sink_mixer(h, positions, w_qkv, q_norm, k_norm, sinks, w_out):
    bsz, s, _ = h.shape
    qkv = h @ w_qkv
    q, k, v = jnp.split(qkv, [AT_HEADS * AT_HEAD_DIM, (AT_HEADS + AT_KV_HEADS) * AT_HEAD_DIM], axis=-1)
    q = q.reshape(bsz, s, AT_HEADS, AT_HEAD_DIM)
    k = k.reshape(bsz, s, AT_KV_HEADS, AT_HEAD_DIM)
    v = v.reshape(bsz, s, AT_KV_HEADS, AT_HEAD_DIM)
    cos, sin = rope_tables(positions)
    q = apply_rope(rms_norm(q, q_norm), cos, sin)
    k = apply_rope(rms_norm(k, k_norm), cos, sin)
    o = banded_sink_attention(q, k, v, sinks)
    return o.astype(h.dtype) @ w_out

def conv_ffn(h, w_up, conv_w, conv_b, w_down):
    g, u = jnp.split(h @ w_up, 2, axis=-1)
    g = causal_dwconv(g, conv_w, conv_b)
    return (jax.nn.gelu(g, approximate=True) * u) @ w_down

def _normal(key, shape, scale):
    return jax.random.normal(key, shape, jnp.float32) * scale

def first_inputs(seed: int = 0) -> dict:
    key = jax.random.key(seed)
    ks = jax.random.split(key, 30)
    x = _normal(ks[0], (BATCH, SEQ, D_MODEL), 1.0)
    p = _normal(ks[1], (DEPTH, BATCH, SEQ, PLE_DIM), 1.0)
    offs = jax.random.randint(ks[2], (BATCH, 1), 0, 1024, dtype=jnp.int32)
    positions = offs + jnp.arange(SEQ, dtype=jnp.int32)[None, :]
    norm_mix = 1.0 + _normal(ks[3], (DEPTH, D_MODEL), 0.05)
    norm_ffn = 1.0 + _normal(ks[4], (DEPTH, D_MODEL), 0.05)
    norm_ple = 1.0 + _normal(ks[5], (DEPTH, D_MODEL), 0.05)
    hy_w_in = _normal(ks[6], (N_EVEN, D_MODEL, HY_IN), D_MODEL ** -0.5)
    hy_b_in = _normal(ks[7], (N_EVEN, HY_IN), 0.02)
    hy_b_in = hy_b_in.at[:, HY_IN - ML_HEADS:].add(jnp.linspace(3.0, 6.0, ML_HEADS))
    rg_conv_w = _normal(ks[8], (N_EVEN, RG_CONV, RG_WIDTH), RG_CONV ** -0.5)
    rg_conv_b = _normal(ks[9], (N_EVEN, RG_WIDTH), 0.02)
    rg_w_a = _normal(ks[10], (N_EVEN, RG_BLOCKS, RG_BLOCK, RG_BLOCK), RG_BLOCK ** -0.5)
    rg_b_a = _normal(ks[11], (N_EVEN, RG_WIDTH), 0.02)
    rg_w_x = _normal(ks[12], (N_EVEN, RG_BLOCKS, RG_BLOCK, RG_BLOCK), RG_BLOCK ** -0.5)
    rg_b_x = _normal(ks[13], (N_EVEN, RG_WIDTH), 0.02)
    a_c = jax.random.uniform(ks[14], (N_EVEN, RG_WIDTH), jnp.float32, 0.9, 0.999)
    a_base = a_c ** (1.0 / RG_C)
    rg_lambda = jnp.log(a_base) - jnp.log1p(-a_base)
    ml_conv_w = _normal(ks[15], (N_EVEN, ML_CONV, 2 * ML_WIDTH), ML_CONV ** -0.5)
    ml_conv_b = _normal(ks[16], (N_EVEN, 2 * ML_WIDTH), 0.02)
    ml_norm = 1.0 + _normal(ks[17], (N_EVEN, ML_WIDTH), 0.05)
    hy_w_out = _normal(ks[18], (N_EVEN, HY_MIX, D_MODEL), HY_MIX ** -0.5)
    at_w_qkv = _normal(ks[19], (N_ODD, D_MODEL, AT_QKV), D_MODEL ** -0.5)
    at_q_norm = 1.0 + _normal(ks[20], (N_ODD, AT_HEAD_DIM), 0.05)
    at_k_norm = 1.0 + _normal(ks[21], (N_ODD, AT_HEAD_DIM), 0.05)
    at_sinks = _normal(ks[22], (N_ODD, AT_HEADS), 0.5)
    at_w_out = _normal(ks[23], (N_ODD, AT_HEADS * AT_HEAD_DIM, D_MODEL), (AT_HEADS * AT_HEAD_DIM) ** -0.5)
    ff_w_up = _normal(ks[24], (DEPTH, D_MODEL, 2 * FF_DIM), D_MODEL ** -0.5)
    ff_conv_w = _normal(ks[25], (DEPTH, FF_CONV, FF_DIM), FF_CONV ** -0.5)
    ff_conv_b = _normal(ks[26], (DEPTH, FF_DIM), 0.02)
    ff_w_down = _normal(ks[27], (DEPTH, FF_DIM, D_MODEL), FF_DIM ** -0.5)
    ple_w_gate = _normal(ks[28], (DEPTH, D_MODEL, D_MODEL), D_MODEL ** -0.5)
    ple_w_proj = _normal(ks[29], (DEPTH, PLE_DIM, D_MODEL), PLE_DIM ** -0.5)
    return {'x': x, 'p': p, 'positions': positions,
            'norm_mix': norm_mix, 'norm_ffn': norm_ffn, 'norm_ple': norm_ple,
            'hy_w_in': hy_w_in, 'hy_b_in': hy_b_in,
            'rg_conv_w': rg_conv_w, 'rg_conv_b': rg_conv_b, 'rg_w_a': rg_w_a, 'rg_b_a': rg_b_a,
            'rg_w_x': rg_w_x, 'rg_b_x': rg_b_x, 'rg_lambda': rg_lambda,
            'ml_conv_w': ml_conv_w, 'ml_conv_b': ml_conv_b, 'ml_norm': ml_norm, 'hy_w_out': hy_w_out,
            'at_w_qkv': at_w_qkv, 'at_q_norm': at_q_norm, 'at_k_norm': at_k_norm, 'at_sinks': at_sinks,
            'at_w_out': at_w_out,
            'ff_w_up': ff_w_up, 'ff_conv_w': ff_conv_w, 'ff_conv_b': ff_conv_b, 'ff_w_down': ff_w_down,
            'ple_w_gate': ple_w_gate, 'ple_w_proj': ple_w_proj}

def first_block(x, p, positions, norm_mix, norm_ffn, norm_ple, hy_w_in, hy_b_in,
              rg_conv_w, rg_conv_b, rg_w_a, rg_b_a, rg_w_x, rg_b_x, rg_lambda,
              ml_conv_w, ml_conv_b, ml_norm, hy_w_out,
              at_w_qkv, at_q_norm, at_k_norm, at_sinks, at_w_out,
              ff_w_up, ff_conv_w, ff_conv_b, ff_w_down, ple_w_gate, ple_w_proj):
    for layer in range(DEPTH):
        h = rms_norm(x, norm_mix[layer])
        if layer % 2 == 0:
            e = layer // 2
            mix = rglru_mlstm_mixer(h, hy_w_in[e], hy_b_in[e], rg_conv_w[e], rg_conv_b[e], rg_w_a[e], rg_b_a[e],
                                    rg_w_x[e], rg_b_x[e], rg_lambda[e], ml_conv_w[e], ml_conv_b[e], ml_norm[e],
                                    hy_w_out[e])
        else:
            o = layer // 2
            mix = swa_sink_mixer(h, positions, at_w_qkv[o], at_q_norm[o], at_k_norm[o], at_sinks[o], at_w_out[o])
        x = x + mix.astype(x.dtype)
        x = x + conv_ffn(rms_norm(x, norm_ffn[layer]), ff_w_up[layer], ff_conv_w[layer], ff_conv_b[layer],
                         ff_w_down[layer]).astype(x.dtype)
        gate = jax.nn.sigmoid(rms_norm(x, norm_ple[layer]) @ ple_w_gate[layer])
        x = x + (gate * (p[layer] @ ple_w_proj[layer])).astype(x.dtype)
    return x


N_MIXERS = 4
MACARON_W = 0.5
D_FF = 2816
ROPE_BASE = 10000.0
REL_BUCKETS = 32
REL_MAX_DIST = 128
MLA_HEADS = 16
MLA_Q_RANK = 384
MLA_KV_RANK = 256
MLA_NOPE = 64
MLA_ROPE = 32
MLA_V = 64
MLA_Q_BLOCK = 128
RWKV_HEAD = 64
RWKV_HEADS = D_MODEL // RWKV_HEAD
RWKV_DECAY_LORA = 64
RWKV_A_LORA = 64
RWKV_GATE_LORA = 160
RWKV_GN_EPS = 64e-5
MOBA_HEADS = 16
MOBA_HEAD_DIM = D_MODEL // MOBA_HEADS
MOBA_BLOCK = 256
MOBA_TOPK = 3
MOBA_Q_CHUNK = 32
RET_HEADS = 4
RET_DK = D_MODEL // RET_HEADS
RET_DV = 2 * D_MODEL // RET_HEADS
RET_CHUNK = 128
RET_GN_EPS = 1e-5


def _rmsnorm(x, g):
    xf = x.astype(jnp.float32)
    y = xf * lax.rsqrt(jnp.mean(xf * xf, axis=-1, keepdims=True) + EPS)
    return (y * g.astype(jnp.float32)).astype(x.dtype)

def _modulate(x, g, shift, scale):
    return _rmsnorm(x, g) * (1 + scale[:, None, :]) + shift[:, None, :]

def _groupnorm_heads(y, w, b, eps):
    B, S, H, N = y.shape
    yf = y.astype(jnp.float32)
    mu = jnp.mean(yf, axis=-1, keepdims=True)
    var = jnp.mean(jnp.square(yf - mu), axis=-1, keepdims=True)
    yn = ((yf - mu) * lax.rsqrt(var + eps)).reshape(B, S, H * N)
    return yn * w.astype(jnp.float32) + b.astype(jnp.float32)

def _swiglu(h, w_in, w_out):
    gt, up = jnp.split(h @ w_in, 2, axis=-1)
    return (jax.nn.silu(gt) * up) @ w_out

def _rope_tables(seq, dim):
    inv = ROPE_BASE ** (-jnp.arange(0, dim, 2, dtype=jnp.float32) / dim)
    ang = jnp.arange(seq, dtype=jnp.float32)[:, None] * inv[None, :]
    return jnp.cos(ang), jnp.sin(ang)

def _apply_rope(x, cos, sin):
    half = x.shape[-1] // 2
    x1 = x[..., :half].astype(jnp.float32)
    x2 = x[..., half:].astype(jnp.float32)
    c = cos[None, :, None, :]
    s = sin[None, :, None, :]
    return jnp.concatenate([x1 * c - x2 * s, x1 * s + x2 * c], axis=-1).astype(x.dtype)

def _t5_bucket(dist):
    n = jnp.maximum(dist, 0)
    max_exact = REL_BUCKETS // 2
    nf = jnp.maximum(n, max_exact).astype(jnp.float32)
    large = max_exact + (jnp.log(nf / max_exact) / math.log(REL_MAX_DIST / max_exact)
                         * (REL_BUCKETS - max_exact)).astype(jnp.int32)
    large = jnp.minimum(large, REL_BUCKETS - 1)
    return jnp.where(n < max_exact, n, large)

def _dense_causal_attention(q, k, v):
    B, S, H, dq = q.shape
    dv = v.shape[-1]
    nq = S // MLA_Q_BLOCK
    qb = q.reshape(B, nq, MLA_Q_BLOCK, H, dq).transpose(1, 0, 3, 2, 4)
    kpos = jnp.arange(S)

    def one_block(args):
        qi, bi = args
        s = jnp.einsum('bhqd,bkhd->bhqk', qi, k).astype(jnp.float32)
        qpos = bi * MLA_Q_BLOCK + jnp.arange(MLA_Q_BLOCK)
        s = jnp.where(kpos[None, :] <= qpos[:, None], s, -jnp.inf)
        p = jax.nn.softmax(s, axis=-1).astype(v.dtype)
        return jnp.einsum('bhqk,bkhd->bqhd', p, v)

    o = lax.map(one_block, (qb, jnp.arange(nq)))
    return o.transpose(1, 0, 2, 3, 4).reshape(B, S, H * dv)

def _mla_mixer(h, w_in, q_norm, w_uq, kv_norm, w_ukv, w_out):
    B, S, _ = h.shape
    H = MLA_HEADS
    cq, ckv, k_rope = jnp.split(h @ w_in, [MLA_Q_RANK, MLA_Q_RANK + MLA_KV_RANK], axis=-1)
    q = (_rmsnorm(cq, q_norm) @ w_uq).reshape(B, S, H, MLA_NOPE + MLA_ROPE)
    kv = (_rmsnorm(ckv, kv_norm) @ w_ukv).reshape(B, S, H, MLA_NOPE + MLA_V)
    cos, sin = _rope_tables(S, MLA_ROPE)
    q = jnp.concatenate([q[..., :MLA_NOPE], _apply_rope(q[..., MLA_NOPE:], cos, sin)], axis=-1)
    k_rope = jnp.broadcast_to(_apply_rope(k_rope[:, :, None, :], cos, sin), (B, S, H, MLA_ROPE))
    k = jnp.concatenate([kv[..., :MLA_NOPE], k_rope], axis=-1)
    v = kv[..., MLA_NOPE:]
    o = _dense_causal_attention(q * (MLA_NOPE + MLA_ROPE) ** -0.5, k, v)
    return o @ w_out

def _rwkv7_mixer(h, mu, w_rkv, w0, wd1, wd2, a0, wa1, wa2, wg1, wg2, k_k, k_a, r_k, gn_w, gn_b, w_out):
    B, S, D = h.shape
    H, N = RWKV_HEADS, RWKV_HEAD
    xx = jnp.pad(h, ((0, 0), (1, 0), (0, 0)))[:, :-1] - h
    xs = h[:, :, None, :] + xx[:, :, None, :] * mu
    rkv = jnp.einsum('bsnd,nde->bsne', xs[:, :, :3], w_rkv)
    r, k, v = rkv[:, :, 0], rkv[:, :, 1], rkv[:, :, 2]
    xw, xa, xg = xs[:, :, 3], xs[:, :, 4], xs[:, :, 5]
    w = -jax.nn.softplus(-(w0 + jnp.tanh(xw @ wd1) @ wd2)) - 0.5
    decay = jnp.exp(-jnp.exp(w.astype(jnp.float32)))
    a = jax.nn.sigmoid((a0 + (xa @ wa1) @ wa2).astype(jnp.float32))
    g = jax.nn.sigmoid(xg @ wg1) @ wg2
    kk = (k * k_k).astype(jnp.float32).reshape(B, S, H, N)
    kk = kk / jnp.maximum(jnp.sqrt(jnp.sum(kk * kk, axis=-1, keepdims=True)), 1e-12)
    k_mod = k.astype(jnp.float32) * (1 + (a - 1) * k_a.astype(jnp.float32))

    def heads(t):
        return t.astype(jnp.float32).reshape(B, S, H, N)

    r_h, k_h, v_h, a_h, w_h = heads(r), heads(k_mod), heads(v), heads(a), heads(decay)

    def tm(t):
        return t.transpose(1, 0, 2, 3)

    def step(state, inp):
        r_t, w_t, k_t, v_t, ka_t, kb_t = inp
        sa = jnp.einsum('bhvk,bhk->bhv', state, ka_t)
        state = (state * w_t[:, :, None, :] + sa[..., None] * kb_t[:, :, None, :]
                 + v_t[..., None] * k_t[:, :, None, :])
        return state, jnp.einsum('bhvk,bhk->bhv', state, r_t)

    state0 = jnp.zeros((B, H, N, N), jnp.float32)
    _, y = lax.scan(step, state0, (tm(r_h), tm(w_h), tm(k_h), tm(v_h), tm(-kk), tm(kk * a_h)))
    y = y.transpose(1, 0, 2, 3)
    yn = _groupnorm_heads(y, gn_w, gn_b, RWKV_GN_EPS)
    bonus = (jnp.sum(r_h * k_h * r_k.astype(jnp.float32), axis=-1, keepdims=True) * v_h).reshape(B, S, D)
    return ((yn + bonus) * g.astype(jnp.float32)).astype(h.dtype) @ w_out

def _moba_mixer(h, w_in, rel_table, w_out):
    B, S, _ = h.shape
    H, dh, BLK, QC = MOBA_HEADS, MOBA_HEAD_DIM, MOBA_BLOCK, MOBA_Q_CHUNK
    qkv = (h @ w_in).reshape(B, S, 3, H, dh)
    q = qkv[:, :, 0].transpose(0, 2, 1, 3) * dh ** -0.5
    k = qkv[:, :, 1].transpose(0, 2, 1, 3)
    v = qkv[:, :, 2].transpose(0, 2, 1, 3)
    nb = -(-S // BLK)
    K = min(MOBA_TOPK, nb)
    pad = nb * BLK - S
    kb = jnp.pad(k, ((0, 0), (0, 0), (0, pad), (0, 0))).reshape(B, H, nb, BLK, dh)
    vb = jnp.pad(v, ((0, 0), (0, 0), (0, pad), (0, 0))).reshape(B, H, nb, BLK, dh)
    kmean = jnp.mean(kb.astype(jnp.float32), axis=3)
    table_t = rel_table.astype(jnp.float32).T
    nc = S // QC
    qc = q.reshape(B, H, nc, QC, dh).transpose(2, 0, 1, 3, 4)
    b_ix = jnp.arange(B)[:, None, None, None]
    h_ix = jnp.arange(H)[None, :, None, None]
    blk_ids = jnp.arange(nb)
    offs = jnp.arange(BLK)

    def chunk(args):
        qi, ci = args
        start = ci * QC
        qpos = start + jnp.arange(QC)
        own = start // BLK
        gate = jnp.einsum('bhqd,bhnd->bhqn', qi.astype(jnp.float32), kmean)
        gate = jnp.where(blk_ids < own, gate, -jnp.inf)
        top_s, top_i = lax.top_k(gate, K)
        valid = jnp.isfinite(top_s)
        k_sel = kb[b_ix, h_ix, top_i]
        v_sel = vb[b_ix, h_ix, top_i]
        pos_sel = top_i[..., None] * BLK + offs
        bias_sel = table_t[h_ix[..., None], _t5_bucket(qpos[:, None, None] - pos_sel)]
        s_sel = jnp.einsum('bhqd,bhqjkd->bhqjk', qi, k_sel).astype(jnp.float32) + bias_sel
        s_sel = jnp.where(valid[..., None], s_sel, -jnp.inf).reshape(B, H, QC, K * BLK)
        k_own = lax.dynamic_index_in_dim(kb, own, axis=2, keepdims=False)
        v_own = lax.dynamic_index_in_dim(vb, own, axis=2, keepdims=False)
        dist_own = qpos[:, None] - (own * BLK + offs)[None, :]
        s_own = jnp.einsum('bhqd,bhkd->bhqk', qi, k_own).astype(jnp.float32) + table_t[:, _t5_bucket(dist_own)]
        s_own = jnp.where(dist_own >= 0, s_own, -jnp.inf)
        p = jax.nn.softmax(jnp.concatenate([s_sel, s_own], axis=-1), axis=-1).astype(v.dtype)
        p_sel = p[..., :K * BLK].reshape(B, H, QC, K, BLK)
        p_own = p[..., K * BLK:]
        return (jnp.einsum('bhqjk,bhqjkd->bhqd', p_sel, v_sel)
                + jnp.einsum('bhqk,bhkd->bhqd', p_own, v_own))

    o = lax.map(chunk, (qc, jnp.arange(nc)))
    o = o.transpose(1, 0, 3, 2, 4).reshape(B, S, H * dh)
    return o @ w_out

def _retnet_mixer(h, w_in, gn_w, gn_b, w_out):
    B, S, D = h.shape
    H, DK, DV, C = RET_HEADS, RET_DK, RET_DV, RET_CHUNK
    q, k, v, g = jnp.split(h @ w_in, [D, 2 * D, 4 * D], axis=-1)
    cos, sin = _rope_tables(S, DK)
    q = _apply_rope(q.reshape(B, S, H, DK), cos, sin).astype(jnp.float32)
    k = _apply_rope(k.reshape(B, S, H, DK) * DK ** -0.5, cos, sin).astype(jnp.float32)
    v = v.reshape(B, S, H, DV).astype(jnp.float32)
    log_gamma = jnp.log1p(-jnp.exp2(-5.0 - jnp.arange(H, dtype=jnp.float32)))
    idx = jnp.arange(C, dtype=jnp.float32)
    diff = idx[:, None] - idx[None, :]
    dmask = jnp.where(diff >= 0, jnp.exp(jnp.maximum(diff, 0.0)[None] * log_gamma[:, None, None]), 0.0)
    zeta = jnp.exp((C - 1 - idx)[None, :] * log_gamma[:, None])
    xi = jnp.exp((idx + 1)[None, :] * log_gamma[:, None])
    gamma_c = jnp.exp(C * log_gamma)
    nc = S // C

    def chunks(t):
        return t.reshape(B, nc, C, H, t.shape[-1]).transpose(1, 0, 3, 2, 4)

    def step(R, inp):
        qc, kc, vc = inp
        inner = jnp.einsum('bhnd,bhmd->bhnm', qc, kc) * dmask
        o = (jnp.einsum('bhnm,bhme->bhne', inner, vc)
             + jnp.einsum('bhnd,bhde->bhne', qc, R) * xi[None, :, :, None])
        R = gamma_c[None, :, None, None] * R + jnp.einsum('bhmd,hm,bhme->bhde', kc, zeta, vc)
        return R, o

    R0 = jnp.zeros((B, H, DK, DV), jnp.float32)
    _, o = lax.scan(step, R0, (chunks(q), chunks(k), chunks(v)))
    o = o.transpose(1, 0, 3, 2, 4).reshape(B, S, H, DV)
    yn = _groupnorm_heads(o, gn_w, gn_b, RET_GN_EPS)
    return (jax.nn.silu(g.astype(jnp.float32)) * yn).astype(h.dtype) @ w_out

def second_inputs(seed: int = 0) -> dict:
    key = jax.random.key(seed)
    ks = iter(jax.random.split(key, 48))
    f32 = jnp.float32

    def nrm(shape, scale):
        return scale * jax.random.normal(next(ks), shape, f32)

    def uni(shape, lo, hi):
        return jax.random.uniform(next(ks), shape, f32, lo, hi)

    D = D_MODEL
    n_mla, n_rwkv, n_moba, n_ret = [len(range(m, DEPTH, N_MIXERS)) for m in range(N_MIXERS)]
    gate_offset = jnp.zeros((3,), f32).at[2].set(1.0)
    return {
        'x': nrm((BATCH, SEQ, D), 1.0),
        'c': nrm((BATCH, D), 1.0),
        'ada_w': nrm((DEPTH, D, 9 * D), 0.2 * D ** -0.5),
        'ada_b': (nrm((DEPTH, 3, 3, D), 0.02) + gate_offset[None, None, :, None]).reshape(DEPTH, 9 * D),
        'norm_g': 1.0 + nrm((DEPTH, 3, D), 0.05),
        'ffn_w_in': nrm((DEPTH, 2, D, 2 * D_FF), D ** -0.5),
        'ffn_w_out': nrm((DEPTH, 2, D_FF, D), D_FF ** -0.5),
        'final_g': 1.0 + nrm((D,), 0.05),
        'rel_table': nrm((REL_BUCKETS, MOBA_HEADS), 0.5),
        'mla_w_in': nrm((n_mla, D, MLA_Q_RANK + MLA_KV_RANK + MLA_ROPE), D ** -0.5),
        'mla_q_norm': 1.0 + nrm((n_mla, MLA_Q_RANK), 0.05),
        'mla_w_uq': nrm((n_mla, MLA_Q_RANK, MLA_HEADS * (MLA_NOPE + MLA_ROPE)), MLA_Q_RANK ** -0.5),
        'mla_kv_norm': 1.0 + nrm((n_mla, MLA_KV_RANK), 0.05),
        'mla_w_ukv': nrm((n_mla, MLA_KV_RANK, MLA_HEADS * (MLA_NOPE + MLA_V)), MLA_KV_RANK ** -0.5),
        'mla_w_out': nrm((n_mla, MLA_HEADS * MLA_V, D), (MLA_HEADS * MLA_V) ** -0.5),
        'rwkv_mu': uni((n_rwkv, 6, D), 0.0, 1.0),
        'rwkv_w_rkv': nrm((n_rwkv, 3, D, D), D ** -0.5),
        'rwkv_w0': uni((n_rwkv, D), -6.5, -1.5),
        'rwkv_wd1': nrm((n_rwkv, D, RWKV_DECAY_LORA), D ** -0.5),
        'rwkv_wd2': nrm((n_rwkv, RWKV_DECAY_LORA, D), 0.5 * RWKV_DECAY_LORA ** -0.5),
        'rwkv_a0': nrm((n_rwkv, D), 0.1),
        'rwkv_wa1': nrm((n_rwkv, D, RWKV_A_LORA), D ** -0.5),
        'rwkv_wa2': nrm((n_rwkv, RWKV_A_LORA, D), RWKV_A_LORA ** -0.5),
        'rwkv_wg1': nrm((n_rwkv, D, RWKV_GATE_LORA), D ** -0.5),
        'rwkv_wg2': nrm((n_rwkv, RWKV_GATE_LORA, D), RWKV_GATE_LORA ** -0.5),
        'rwkv_k_k': 0.85 + nrm((n_rwkv, D), 0.05),
        'rwkv_k_a': 1.0 + nrm((n_rwkv, D), 0.05),
        'rwkv_r_k': nrm((n_rwkv, RWKV_HEADS, RWKV_HEAD), 0.1),
        'rwkv_gn_w': 1.0 + nrm((n_rwkv, D), 0.05),
        'rwkv_gn_b': nrm((n_rwkv, D), 0.02),
        'rwkv_w_out': nrm((n_rwkv, D, D), D ** -0.5),
        'moba_w_in': nrm((n_moba, D, 3 * D), D ** -0.5),
        'moba_w_out': nrm((n_moba, D, D), D ** -0.5),
        'ret_w_in': nrm((n_ret, D, 6 * D), D ** -0.5),
        'ret_gn_w': 1.0 + nrm((n_ret, 2 * D), 0.05),
        'ret_gn_b': nrm((n_ret, 2 * D), 0.02),
        'ret_w_out': nrm((n_ret, 2 * D, D), (2 * D) ** -0.5),
    }

def second_block(x, c, ada_w, ada_b, norm_g, ffn_w_in, ffn_w_out, final_g, rel_table,
              mla_w_in, mla_q_norm, mla_w_uq, mla_kv_norm, mla_w_ukv, mla_w_out,
              rwkv_mu, rwkv_w_rkv, rwkv_w0, rwkv_wd1, rwkv_wd2, rwkv_a0, rwkv_wa1, rwkv_wa2,
              rwkv_wg1, rwkv_wg2, rwkv_k_k, rwkv_k_a, rwkv_r_k, rwkv_gn_w, rwkv_gn_b, rwkv_w_out,
              moba_w_in, moba_w_out, ret_w_in, ret_gn_w, ret_gn_b, ret_w_out):
    B = x.shape[0]
    c_act = jax.nn.silu(c)
    for i in range(DEPTH):
        mods = (c_act @ ada_w[i] + ada_b[i]).reshape(B, 3, 3, D_MODEL)
        h = _modulate(x, norm_g[i, 0], mods[:, 0, 0], mods[:, 0, 1])
        x = x + MACARON_W * mods[:, 0, 2][:, None, :] * _swiglu(h, ffn_w_in[i, 0], ffn_w_out[i, 0])
        h = _modulate(x, norm_g[i, 1], mods[:, 1, 0], mods[:, 1, 1])
        kind, j = i % N_MIXERS, i // N_MIXERS
        if kind == 0:
            y = _mla_mixer(h, mla_w_in[j], mla_q_norm[j], mla_w_uq[j], mla_kv_norm[j], mla_w_ukv[j], mla_w_out[j])
        elif kind == 1:
            y = _rwkv7_mixer(h, rwkv_mu[j], rwkv_w_rkv[j], rwkv_w0[j], rwkv_wd1[j], rwkv_wd2[j], rwkv_a0[j],
                             rwkv_wa1[j], rwkv_wa2[j], rwkv_wg1[j], rwkv_wg2[j], rwkv_k_k[j], rwkv_k_a[j],
                             rwkv_r_k[j], rwkv_gn_w[j], rwkv_gn_b[j], rwkv_w_out[j])
        elif kind == 2:
            y = _moba_mixer(h, moba_w_in[j], rel_table, moba_w_out[j])
        else:
            y = _retnet_mixer(h, ret_w_in[j], ret_gn_w[j], ret_gn_b[j], ret_w_out[j])
        x = x + mods[:, 1, 2][:, None, :] * y
        h = _modulate(x, norm_g[i, 2], mods[:, 2, 0], mods[:, 2, 1])
        x = x + MACARON_W * mods[:, 2, 2][:, None, :] * _swiglu(h, ffn_w_in[i, 1], ffn_w_out[i, 1])
    return _rmsnorm(x, final_g)


def setup_inputs(seed=0):
    out = dict(first_inputs(seed))
    for name, value in second_inputs(seed + 1).items():
        if name != "x":
            out[name + "_2"] = value
    return out


def reference(
    x, p, positions, norm_mix, norm_ffn, norm_ple, hy_w_in, hy_b_in, rg_conv_w, rg_conv_b,
    rg_w_a, rg_b_a, rg_w_x, rg_b_x, rg_lambda, ml_conv_w, ml_conv_b, ml_norm, hy_w_out,
    at_w_qkv, at_q_norm, at_k_norm, at_sinks, at_w_out, ff_w_up, ff_conv_w, ff_conv_b,
    ff_w_down, ple_w_gate, ple_w_proj, c_2, ada_w_2, ada_b_2, norm_g_2, ffn_w_in_2, ffn_w_out_2,
    final_g_2, rel_table_2, mla_w_in_2, mla_q_norm_2, mla_w_uq_2, mla_kv_norm_2, mla_w_ukv_2,
    mla_w_out_2, rwkv_mu_2, rwkv_w_rkv_2, rwkv_w0_2, rwkv_wd1_2, rwkv_wd2_2, rwkv_a0_2,
    rwkv_wa1_2, rwkv_wa2_2, rwkv_wg1_2, rwkv_wg2_2, rwkv_k_k_2, rwkv_k_a_2, rwkv_r_k_2,
    rwkv_gn_w_2, rwkv_gn_b_2, rwkv_w_out_2, moba_w_in_2, moba_w_out_2, ret_w_in_2, ret_gn_w_2,
    ret_gn_b_2, ret_w_out_2,
):
    x = first_block(
        x, p, positions, norm_mix, norm_ffn, norm_ple, hy_w_in, hy_b_in, rg_conv_w, rg_conv_b,
        rg_w_a, rg_b_a, rg_w_x, rg_b_x, rg_lambda, ml_conv_w, ml_conv_b, ml_norm, hy_w_out,
        at_w_qkv, at_q_norm, at_k_norm, at_sinks, at_w_out, ff_w_up, ff_conv_w, ff_conv_b,
        ff_w_down, ple_w_gate, ple_w_proj,
    )
    return second_block(
        x, c_2, ada_w_2, ada_b_2, norm_g_2, ffn_w_in_2, ffn_w_out_2, final_g_2, rel_table_2,
        mla_w_in_2, mla_q_norm_2, mla_w_uq_2, mla_kv_norm_2, mla_w_ukv_2, mla_w_out_2,
        rwkv_mu_2, rwkv_w_rkv_2, rwkv_w0_2, rwkv_wd1_2, rwkv_wd2_2, rwkv_a0_2, rwkv_wa1_2,
        rwkv_wa2_2, rwkv_wg1_2, rwkv_wg2_2, rwkv_k_k_2, rwkv_k_a_2, rwkv_r_k_2, rwkv_gn_w_2,
        rwkv_gn_b_2, rwkv_w_out_2, moba_w_in_2, moba_w_out_2, ret_w_in_2, ret_gn_w_2,
        ret_gn_b_2, ret_w_out_2,
    )


_drawn_inputs = setup_inputs


def setup_inputs(seed=0):
    import zlib

    import numpy as np

    out = dict(_drawn_inputs(seed))
    spreads = {}
    factors = {'norm_ple': 4.528,
     'rg_b_a': 8.0,
     'rg_b_x': 8.0,
     'ml_conv_b': 6.232,
     'at_q_norm': 8.0,
     'at_k_norm': 8.0,
     'at_sinks': 4.555,
     'ff_conv_b': 3.777,
     'mla_q_norm_2': 8.0,
     'mla_kv_norm_2': 4.984,
     'rwkv_wd1_2': 5.166,
     'rwkv_wd2_2': 4.75,
     'rwkv_a0_2': 4.839,
     'rwkv_gn_w_2': 12.382,
     'rwkv_gn_b_2': 29.003,
     'rwkv_k_k_2': 2.773,
     'rwkv_r_k_2': 3.326}
    for name, (base, spread) in spreads.items():
        noise = np.random.default_rng([zlib.crc32(name.encode()), seed]).standard_normal(out[name].shape)
        drawn = base * np.exp(spread * noise) if base else spread * noise
        out[name] = jnp.asarray(drawn.astype(out[name].dtype))
    for name, factor in factors.items():
        out[name] = (out[name] * factor).astype(out[name].dtype)
    return out
```

```python
from contextlib import ExitStack

import numpy as np

import concourse.bass as bass
from concourse import mybir

F32 = mybir.dt.float32
I32 = mybir.dt.int32
ALU = mybir.AluOpType
ACT = mybir.ActivationFunctionType
AX = mybir.AxisListType.X

P = 128
T = 512
NB = T // P
DB = 1024 // P
RING = 3
TILE = 16
TURN = 96
EPS = 1e-6
RG_C = 8.0
FF1, FF2 = 3072 // P, 2816 // P
HEADS, KV = 16, 4
LORA_G = 160
DECAY = float(np.exp(-0.5))

STAGES = []


def stage(name, products, smalls, blocks):
    STAGES.append((name, products, smalls, blocks))


def first_ffn(n):
    stage(f"norm{n}", 0, 1, 0)
    stage(f"up{n}", 2 * FF1 + 16, 0, 2 * 2 * FF1 * DB)
    stage(f"down{n}", DB + 8, 0, 2 * DB * FF1)


def second_ffn(n):
    stage(f"norm{n}", 0, 1, 0)
    stage(f"up{n}", 2 * FF2, 0, 2 * FF2 * DB)
    stage(f"down{n}", DB, 0, DB * FF2)


def ple(n):
    stage(f"norm{n}", 0, 1, 0)
    stage(f"ple{n}", 2 * DB, 0, DB * (DB + 2))


stage("norm0", 0, 1, 0)
stage("hy_in", 12 + 4 + 4 + 2 + 4, 0, 12 * DB + 8 * DB + 8 + 4 * DB)
stage("rg", 0, 8, 0)
stage("ml", 0, 1 + 8 + 4 * 7, 0)
stage("hy_out", DB, 0, DB * DB)
first_ffn(1)
ple(2)
stage("norm3", 0, 1, 0)
stage("at_in", 12 + 4, 2 * 12, 12 * DB + 2 * DB)
stage("at", 0, 32 * 3, 0)
stage("at_out", DB, 0, DB * DB)
first_ffn(4)
ple(5)
second_ffn(6)
stage("norm7", 0, 1, 0)
stage("mla_in", 6, 3, 6 * DB)
stage("mla_q", 16, 16, 3 * 16)
stage("mla_k", 16, 0, 16)
stage("mla_v", 8, 0, 16)
stage("mla", 0, 16 * 9, 0)
stage("mla_out", DB, 0, DB * DB)
second_ffn(8)
second_ffn(9)
stage("norm10", 0, 1, 0)
stage("rw_in", 24 + 2 + 16 + 2, 0, 24 * DB + 2 * DB + 16 + 2 * DB)
stage("rw_prep", 0, 16, 0)
stage("rw", 0, 36 * 16, 0)
stage("rw_g", 8, 16, 16)
stage("rw_out", DB, 0, DB * DB)
second_ffn(11)
stage("norm12", 0, 1, 0)


def starts():
    at, m, s, w = {}, 0, 0, 0
    for name, products, smalls, blocks in STAGES:
        at[name] = (m, s, w)
        m, s, w = m + products, s + smalls, w + blocks
    at["end"] = (m, s, w)
    return at


AT = starts()
TILES = -(-AT["end"][2] // TILE)

VECTORS = {
    "norm_mix": 16, "norm_ffn": 16, "norm_ple": 16,
    "hy_b": 26, "rg_conv_w": 16, "rg_conv_b": 4, "rg_b_a": 4, "rg_b_x": 4, "rg_lambda": 4,
    "ml_conv_w": 32, "ml_conv_b": 8, "ml_norm": 4,
    "ff_conv_w": 2 * 3 * FF1, "ff_conv_b": 2 * FF1, "at_q_norm": 1, "at_k_norm": 1, "at_sinks": 16,
    "norm_g": 48, "ada_b": 144, "final_g": 8, "mla_q_norm": 3, "mla_kv_norm": 2,
    "rwkv_mu": 48, "rwkv_w0": 8, "rwkv_a0": 8, "rwkv_k_k": 8, "rwkv_k_a": 8, "rwkv_r_k": 8,
    "rwkv_gn_w": 8, "rwkv_gn_b": 8, "c": 8, "inv_freq": 1, "eps": 1, "gn_eps": 1,
}
VAT, NV = {}, 0
for _name, _n in VECTORS.items():
    VAT[_name] = NV
    NV += _n

CONSTS = {"ident": 128, "ones": 128, "halves": 128, "turn": 128, "turn_mla": 128, "upto": 128,
          "before_t": 128, "before": 128, "level": 7 * 128, "level0_t": 128, "sel": 512,
          "band": 256, "causal": 512}
CAT, NC = {}, 0
for _name, _n in CONSTS.items():
    CAT[_name] = NC
    NC += _n


def constants():
    c = {}
    i = np.arange(P)
    c["ident"] = np.eye(P)
    c["ones"] = np.ones((P, P))
    c["halves"] = (i[:, None] // 64 == i[None, :] // 64) * 1.0
    turn = np.zeros((P, P))
    for j in range(P):
        turn[j + 32 if j % 64 < 32 else j - 32, j] = -1.0 if j % 64 < 32 else 1.0
    c["turn"] = turn
    turn = np.zeros((P, P))
    for j in range(64, 96):
        turn[j + 16 if j < 80 else j - 16, j] = -1.0 if j < 80 else 1.0
    c["turn_mla"] = turn
    c["upto"] = (i[:, None] <= i[None, :]) * 1.0
    c["before_t"] = (i[:, None] < i[None, :]) * 1.0
    c["before"] = (i[:, None] > i[None, :]) * 1.0
    c["level"] = np.concatenate([((i[:, None] >> n) % 2 == 1) * ((i[None, :] >> n) == (i[:, None] >> n) - 1)
                                 for n in range(7)], axis=1) * 1.0
    c["level0_t"] = c["level"][:, :P].T
    sel = np.zeros((P, 4, P))
    for h in range(4):
        sel[h, h, :] = 1.0
    c["sel"] = sel.reshape(P, 512)
    k = np.arange(2 * P)
    band = (k[None, :] > i[:, None]) & (k[None, :] <= i[:, None] + P)
    c["band"] = np.where(band, 0.0, -1e30)
    causal = np.zeros((P, 512))
    causal[:, 384:] = np.where(i[None, :] <= i[:, None], 0.0, -1e30)
    c["causal"] = causal
    return np.concatenate([c[n] for n in CONSTS], axis=1).astype(np.float32)


def build(nc, io):
    with ExitStack() as ctx:
        def sb(name, *shape):
            return ctx.enter_context(nc.sbuf_tensor(name, [P, *shape], F32))

        names = {}

        def S(name):
            if name not in names:
                names[name] = ctx.enter_context(nc.semaphore(name))
            return names[name]

        X = sb("residual", DB, T)
        H = sb("normed", DB, T)
        A = sb("area_a", 24, T)
        B = sb("area_b", 24, T)
        ring = sb("weight_ring", RING, TILE * P)
        TM = sb("temporary", 4, T)
        SQ = sb("squares", 2, T)
        RB = sb("rstd", T)
        PT = sb("per_layer_input", 2, T)
        RW = sb("rwkv_matrices", 5, T)
        V = sb("vector_columns", NV, 1)
        C = sb("constant_matrices", NC)
        MODS = sb("modulations", 144, 1)
        GS = sb("modulated_gains", 48, 1)
        SM = sb("small_columns", 96)
        SC = sb("rwkv_scratch", 1536)
        SA = sb("rwkv_scaled", 2, T)
        bank = [ctx.enter_context(nc.psum_tensor(f"bank{b}", [P, T], F32)) for b in range(8)]

        def vec(name, j):
            return V[:, VAT[name] + j, :]

        def const(name, j=0, n=P):
            return C[:, CAT[name] + j * n:CAT[name] + (j + 1) * n]

        product_full, small_full = S("product_full"), S("small_full")
        product_done = [S(f"product_done{b}") for b in range(4)]
        small_done = [S(f"small_done{b}") for b in range(4)]

        def pbank(m):
            return bank[m % 4]

        def sbank(s):
            return bank[4 + s % 4]

        def full(eng, m, more=0):
            eng.wait_ge(product_full, more + (m + 1))

        def done(eng, m, rounds=0):
            eng.wait_ge(product_done[m % 4], rounds + (m // 4 + 1))

        def sfull(eng, s):
            eng.wait_ge(small_full, s + 1)

        def sdone(eng, s):
            eng.wait_ge(small_done[s % 4], s // 4 + 1)

        landed = [S(f"tile_landed{j}") for j in range(RING)]
        tile_used = S("tile_used")
        X_T = io["x"]
        UPDATE = {1: "hy_out", 2: "down1", 3: "ple2", 4: "at_out", 5: "down4", 6: "ple5", 7: "down6",
                  8: "mla_out", 9: "down8", 10: "down9", 11: "rw_out", 12: "down11"}

        def update(n, k):
            m = AT[UPDATE[n]][0]
            name = UPDATE[n]
            return m + (2 * k + 1 if name.startswith("ple") else 2 * k if name in ("down1", "down4") else k)

        def up_product(n, f):
            return AT[f"up{n}"][0] + 16 * (f // 12) + f % 12 + f % 12 // 3

        AT_ORDER = {}
        LAG = 3
        for u in range(32 + LAG + 1):
            for what, v in (("scores", u), ("turned", u - LAG), ("output", u - LAG - 1)):
                if 0 <= v < 32:
                    AT_ORDER[what, v] = len(AT_ORDER)

        def at_small(what, v):
            return AT["at"][1] + AT_ORDER[what, v]

        def gn_small(what, j):
            return AT["rw_g"][1] + ((2 * j - 1 if j else 0) if what == "mean" else 2 * j + 2 - (j == DB - 1))

        def at_in_small(what, b):
            s = AT["at_in"][1]
            return s + ((2 * b - 1 if b else 0) if what == "sum" else 2 * b + 2 - (b == 11))

        MLA_ORDER = {}
        MLAG = 3
        for u in range(16 * NB + MLAG):
            if u < 16 * NB:
                MLA_ORDER["scores", u] = len(MLA_ORDER)
            if u >= MLAG:
                MLA_ORDER["turned", u - MLAG] = len(MLA_ORDER)
                if (u - MLAG) % NB == NB - 1:
                    MLA_ORDER["output", (u - MLAG) // NB] = len(MLA_ORDER)

        def mla_small(what, u):
            return AT["mla"][1] + MLA_ORDER[what, u]

        STEPS = [(c, g) for c in range(NB) for g in range(4)]
        scaled_of = [x.rearrange("p a (b t) -> p (a b) t", t=P) for x in (TM[:, 0:2, :], SA[:, :, :])]
        tok = TM[:, 2:4, :].rearrange("p a (b t) -> p (a b) t", t=P)
        Z = tok[:, 6:8, :].rearrange("p a (b v) -> p (a b) v", v=64)
        INV, INVT = SQ[:, 0, :], SQ[:, 1, :]
        LOW = SC[:, 0:512]
        U = SC[:, 512:768].rearrange("p (b v) -> p b v", v=64)
        GROW = SC[:, 768:1026].rearrange("p (b t) -> p b t", t=129)
        SHRINK = SC[:, 1026:1282].rearrange("p (b t) -> p b t", t=P)
        START = SC[:, 1282:1410].rearrange("p (b v) -> p b v", v=64)
        STATE = RB[:, :].rearrange("p (b v) -> p b v", v=64)
        DV, DN = SM[:, 48:50], SM[:, 50:52]
        DS = [SM[:, 52:54], SM[:, 54:56]]

        def decay_end(c, g):
            return SM[:, 62 + 8 * (c % 2) + 2 * g:64 + 8 * (c % 2) + 2 * g]

        RW_ORDER = []
        FILL = {0: [("matrix", 4), ("turned", 1)], 1: [("matrix", 5), ("turned", 0)], 2: [("matrix", 6), ("z", 0)],
                3: [("matrix", 7), ("z", 1)], 4: [("matrix", 8)], 5: [("matrix", 9)]}
        for lv in range(6):
            RW_ORDER += [("low", lv), *FILL[lv], *([("inv", lv)] if lv < 5 else []), ("invt", lv)]
        RW_TAIL = [("u", 0), ("y", 0), ("y", 1), ("state", 0), ("state", 1)]
        RW_AT = {}
        for j in range(4):
            RW_AT[0, "matrix", j] = len(RW_AT)
        for i in range(len(STEPS)):
            for what, j in RW_ORDER:
                RW_AT[i, what, j] = len(RW_AT)
            for j in range(4 if i + 1 < len(STEPS) else 0):
                RW_AT[i + 1, "matrix", j] = len(RW_AT)
            for what, j in RW_TAIL:
                RW_AT[i, what, j] = len(RW_AT)
        MATRICES = ((0, 4), (4, 0), (6, 0), (4, 2), (6, 2))
        MASKS = ("before", "before_t", "before_t", "upto", "upto")

        def rw_small(step, what, j=0):
            return AT["rw"][1] + RW_AT[step, what, j]

        block = ctx.enter_context(nc.Block())

        @block.sync
        def _(sp):
            tiles = io["weights"]
            for n in range(6):
                if n >= RING:
                    sp.wait_ge(tile_used, n - RING + 1)
                sp.dma_start(ring[:, n % RING, :], tiles[n]).then_inc(landed[n % RING], 16)
            with sp.Fori(1, TILES // 6) as i:
                for n in range(6):
                    sp.wait_ge(tile_used, i * 6 + (n - RING + 1))
                    sp.dma_start(ring[:, n % RING, :], tiles[i * 6 + n]).then_inc(landed[n % RING], 16)
            for n in range(TILES // 6 * 6, TILES):
                sp.wait_ge(tile_used, n - RING + 1)
                sp.dma_start(ring[:, n % RING, :], tiles[n]).then_inc(landed[n % RING], 16)
            sp.wait_ge(S("result_ready"), DB)
            sp.dma_start(io["out"].rearrange("(k p) t -> p k t", p=P), H[:, :, :]).then_inc(S("result_stored"), 16)
            sp.wait_ge(S("result_stored"), 16)

        @block.gpsimd
        def _(po):
            po.dma_start(X[:, :, :], X_T.rearrange("(k p) t -> p k t", p=P)).then_inc(S("x_landed"), 16)
            po.dma_start(V[:, :, :], io["vectors"]).then_inc(S("vectors_landed"), 16)
            po.dma_start(C[:, :], io["constants"]).then_inc(S("constants_landed"), 16)
            po.dma_start(B[:, 0:2, :], io["rg_blocks"]).then_inc(S("rg_blocks_landed"), 16)
            po.dma_start(RW[:, 0, :], io["v_bias"]).then_inc(S("v_bias_landed"), 16)
            po.dma_start(PT[:, :, :], io["p"][0]).then_inc(S("p0_landed"), 16)
            for h in range(4):
                for j in range(NB):
                    po.wait_ge(S("ml_exp"), 4 * h + j + 1)
                    w = B[:, 12 + 4 * (h % 2) + j, j * P:(j + 1) * P]
                    po.tensor_tensor(w, w, const("upto"), ALU.mult).then_inc(S("ml_masked"), 1)
            for k in range(DB):
                done(po, update(3, k))
            po.dma_start(PT[:, :, :], io["p"][1]).then_inc(S("p1_landed"), 16)
            po.dma_start(B[:, 2, :].bitcast(I32), io["positions"]).then_inc(S("positions_landed"), 16)
            for k in range(DB):
                done(po, update(6, k))
            po.dma_start(B[:, 22:24, :], io["mla_tables"]).then_inc(S("mla_tables_landed"), 16)
            po.wait_ge(S("mla_key"), 1)
            po.tensor_copy(B[64:96, 0:16, :], B[64:96, 21:22, :].to_broadcast([32, 16, T]))\
                .then_inc(S("mla_keys_spread"), 1)

        @block.tensor
        def _(pe):
            at = {"m": 0, "s": 0, "w": 0, "free_inc": False, "turn": 0}

            def mm(out, lhsT, rhs, start, stop, inc=None):
                i = pe.matmul(out, lhsT, rhs, start=start, stop=stop)
                if inc is not None:
                    i.then_inc(inc, 1)
                elif at["free_inc"]:
                    i.then_inc(tile_used, 1)
                    at["free_inc"] = False

            def weight(n=1):
                w = at["w"]
                slot = w // TILE % RING
                if w % TILE == 0:
                    at["free_inc"] = w > 0
                    pe.wait_ge(landed[slot], at["turn"] * (16 * 6 // RING) + 16 * (w // TILE // RING + 1))
                at["w"] = w + n
                return ring[:, slot, w % TILE * P:(w % TILE + n) * P]

            def product(rounds=0):
                m = at["m"]
                at["m"] += 1
                if m >= 4 or not isinstance(rounds, int):
                    pe.wait_ge(product_done[m % 4], rounds + m // 4)
                return m

            def small():
                s = at["s"]
                at["s"] += 1
                if s >= 4:
                    pe.wait_ge(small_done[s % 4], s // 4)
                return s

            def begin(name):
                assert (at["m"], at["s"], at["w"]) == AT[name], (name, at, AT[name])

            def loop(n, products, body, turns=1):
                m, w, f = at["m"], at["w"], at["free_inc"]
                with pe.Fori(0, n) as i:
                    at["turn"] = i * turns
                    body(i)
                    assert at["w"] == w + turns * TURN and at["m"] == m + products and at["free_inc"] == f
                at["turn"] = 0
                at["m"], at["w"] = m + n * products, w + n * turns * TURN

            def norm_sum(n):
                begin(f"norm{n}")
                s = small()
                for k in range(DB):
                    pe.wait_ge(S("square_ready"), DB * n + k + 1)
                    mm(sbank(s)[:, :], const("ones"), SQ[:, k % 2, :], k == 0, k == DB - 1,
                       small_full if k == DB - 1 else S("square_used"))

            def project(rhs, kb, ready, cols=P, rows=P, rounds=0):
                m = product(rounds)
                for k in range(kb):
                    ready(k)
                    mm(pbank(m)[0:cols, :], weight()[0:rows, 0:cols], rhs(k)[0:rows, :], k == 0, k == kb - 1,
                       product_full if k == kb - 1 else None)
                return m

            def normed(n):
                return lambda k: pe.wait_ge(S("normed_ready"), DB * n + k + 1)

            def settled(k):
                pass

            def token_major(rhs_of, kb, cols, ready):
                ms = []
                for k in range(kb):
                    ready(k)
                    w = weight(cols // P)
                    for t in range(NB):
                        if k == 0:
                            ms.append(product())
                        mm(pbank(ms[t])[:, 0:cols], rhs_of(k)[:, t * P:(t + 1) * P], w, k == 0, k == kb - 1,
                           product_full if k == kb - 1 else None)
                return ms

            def columns(rounds):
                m = product(rounds=rounds)
                for j in range(3):
                    for k in range(DB):
                        mm(pbank(m)[:, j:j + 1], weight(), SM[:, 80 + k:81 + k], k == 0, k == DB - 1,
                           product_full if j == 2 and k == DB - 1 else None)

            def up_conv(n):
                begin(f"up{n}")
                pe.wait_ge(S("c_act"), 1)

                def body(i):
                    for j in range(12):
                        project(lambda k: H[:, k, :], DB, normed(n) if j == 0 else settled, rounds=i * 4)
                        if j % 3 == 2:
                            columns(i * 4)
                loop(4, 16, body, turns=2)

            def down_conv(n):
                begin(f"down{n}")

                def body(i):
                    for j in range(4):
                        project(lambda k: A[:, k, :], FF1, (lambda k: done(pe, up_product(n, 2 * k + 1))) if j == 0 else settled,
                                rounds=i * 2)
                        columns(i * 2)
                loop(2, 8, body, turns=2)

            def up(n, laps, rest):
                begin(f"up{n}")
                h = lambda k: H[:, k, :]
                if laps:
                    def body(i):
                        for j in range(12):
                            project(h, DB, normed(n), rounds=i * 3)
                    loop(laps, 12, body)
                for j in range(rest):
                    project(h, DB, settled)

            def down(n, kb):
                begin(f"down{n}")
                m0 = AT[f"up{n}"][0]
                a = lambda k: A[:, k, :]
                hidden = lambda k: done(pe, m0 + 2 * k + 1)
                for j in range(DB):
                    project(a, kb, hidden if j == 0 else settled)

            def ple(n):
                norm_sum(n)
                begin(f"ple{n}")
                for j in range(DB):
                    project(lambda k: H[:, k, :], DB, normed(n) if j == 0 else settled)
                    project(lambda k: PT[:, k, :], 2,
                            (lambda k: pe.wait_ge(S(f"p{n // 3}_landed"), 16)) if j == 0 else settled)

            pe.wait_ge(S("constants_landed"), 16)
            norm_sum(0)
            begin("hy_in")
            h = lambda k: H[:, k, :]
            for j in range(20):
                project(h, DB, normed(0) if j == 0 else settled)
            mi, mf = product(), product()
            for k in range(DB):
                w = weight()
                mm(pbank(mi)[0:4, :], w[:, 0:4], h(k), k == 0, k == DB - 1, product_full if k == DB - 1 else None)
                mm(pbank(mf)[0:4, :], w[:, 4:8], h(k), k == 0, k == DB - 1, product_full if k == DB - 1 else None)
            token_major(h, DB, T, settled)
            begin("rg")
            pe.wait_ge(S("rg_blocks_landed"), 16)
            for j in range(4):
                pe.wait_ge(S("conv_done"), j + 1)
                for g in range(2):
                    s = small()
                    mm(sbank(s)[:, :], B[:, g, j * P:(j + 1) * P], B[:, 4 + j, :], True, True, small_full)
            begin("ml")
            pe.wait_ge(S("gate_rows"), 2)
            s = small()
            for t in range(NB):
                i = pe.transpose(sbank(s)[:, 4 * t:4 * t + 4], A[0:4, 20, t * P:(t + 1) * P], const("ident")[0:4, 0:4])
            i.then_inc(small_full, 1)
            for row in (23, 22):
                for hd in range(4):
                    s = small()
                    mm(sbank(s)[:, :], C[0:4, CAT["sel"] + hd * P:CAT["sel"] + (hd + 1) * P],
                       A[0:4, row, :], True, True, small_full)
            pe.wait_ge(S("qk_ready"), 1)
            for hd in range(4):
                ss = []
                for j in range(NB):
                    s = small()
                    ss.append(s)
                    mm(sbank(s)[:, j * P:], A[:, 4 + hd, j * P:(j + 1) * P], A[:, hd, j * P:], True, True, small_full)
                for what in range(2):
                    s = small()
                    for j in range(NB):
                        if what == 0:
                            sdone(pe, ss[j])
                            done(pe, AT["hy_in"][0] + 22 + j)
                        mm(sbank(s)[:, j * P:], A[:, 16 + j, hd * P:(hd + 1) * P] if what == 0 else const("ones"),
                           B[:, 12 + 4 * (hd % 2) + j, j * P:], j == 0, j == NB - 1, small_full if j == NB - 1 else None)
                s = small()
                pe.wait_ge(S("ml_square"), hd + 1)
                mm(sbank(s)[:, :], const("ones"), SQ[:, 0, :], True, True, small_full)
            begin("hy_out")
            pe.wait_ge(S("y_rg"), 1)
            y = lambda k: B[:, 20 + k, :] if k < 4 else B[:, k - 4, :]
            for j in range(DB):
                project(y, DB, (lambda k: pe.wait_ge(S("y_ml"), max(1, k - 3))) if j == 0 else settled)
            norm_sum(1)
            up_conv(1)
            down_conv(1)
            ple(2)

            norm_sum(3)
            begin("at_in")

            for j in range(12 + 2):
                if j < 12:
                    project(h, DB, normed(3) if j == 0 else settled)
                if j >= 1 and j <= 12:
                    s = small()
                    pe.wait_ge(S("at_square"), j)
                    mm(sbank(s)[:, :], const("halves"), SQ[:, (j - 1) % 2, :], True, True, small_full)
                if j >= 2:
                    s = small()
                    pe.wait_ge(S("at_scaled"), j - 1)
                    mm(sbank(s)[:, :], const("turn"), A[:, j - 2, :], True, True, small_full)
            token_major(h, DB, 256, settled)
            begin("at")
            s0 = at["s"]
            pe.wait_ge(S("at_rotated"), 12)
            for t in range(NB):
                done(pe, AT["at_in"][0] + 12 + t)
            for u in range(32 + LAG + 1):
                if u < 32:
                    n, g, half = u // 8, u // 2 % 4, u % 2
                    rows = slice(64 * half, 64 * half + 64)
                    s = small()
                    for e in range(2):
                        keys = slice((n - 1) * P, (n + 1) * P) if n else slice(0, P)
                        mm(sbank(s)[:, 256 * e + (0 if n else 128):256 * e + 256], A[rows, 2 * g + e, n * P:(n + 1) * P],
                           A[rows, 8 + g, keys], True, True, small_full if e == 1 else None)
                if 0 <= u - LAG < 32:
                    v = u - LAG
                    s = small()
                    pe.wait_ge(S("at_probs"), v + 1)
                    for e in range(2):
                        for b in range(0 if v >= 8 else 1, 2):
                            i = pe.transpose(sbank(s)[:, (2 * e + b) * P:(2 * e + b + 1) * P],
                                             TM[:, v % 4, (2 * e + b) * P:(2 * e + b + 1) * P], const("ident"))
                    i.then_inc(small_full, 1)
                if u >= LAG + 1:
                    v = u - LAG - 1
                    n, g, half = v // 8, v // 2 % 4, v % 2
                    s = small()
                    sdone(pe, at_small("turned", v))
                    for e in range(2):
                        for b in range(0 if n else 1, 2):
                            at_tokens = n - 1 + b
                            mm(sbank(s)[64 * half:64 * half + 64, e * P:(e + 1) * P],
                               A[:, 12 + at_tokens // 2, at_tokens % 2 * 256 + 64 * g:at_tokens % 2 * 256 + 64 * g + 64],
                               B[:, 12 + v % 4, (2 * e + b) * P:(2 * e + b + 1) * P], b == (0 if n else 1), b == 1,
                               small_full if e == 1 and b == 1 else None)
            begin("at_out")
            for v in range(28, 32):
                sdone(pe, at_small("output", v))
            for j in range(DB):
                project(lambda k: B[:, 4 + k, :], DB, settled)
            norm_sum(4)
            up_conv(4)
            down_conv(4)
            ple(5)
            norm_sum(6)
            up(6, 3, 8)
            down(6, FF2)
            norm_sum(7)
            begin("mla_in")
            for j in range(6):
                project(h, DB, normed(7) if j == 0 else settled)
            for j0, n in ((0, 3), (3, 2)):
                s = small()
                for j in range(n):
                    pe.wait_ge(S("mla_square"), j0 + j + 1)
                    mm(sbank(s)[:, :], const("ones"), SQ[:, (j0 + j) % 2, :], j == 0, j == n - 1,
                       small_full if j == n - 1 else S("mla_square_used"))
            s = small()
            done(pe, AT["mla_in"][0] + 5)
            mm(sbank(s)[:, :], const("turn_mla"), B[:, 21, :], True, True, small_full)
            begin("mla_q")
            for j in range(17):
                if j < 16:
                    project(lambda k: B[:, 16 + k, :], 3,
                            (lambda k: pe.wait_ge(S("mla_normed"), k + 1)) if j == 0 else settled, cols=96)
                if j >= 1:
                    s = small()
                    done(pe, AT["mla_q"][0] + j - 1)
                    mm(sbank(s)[0:96, :], const("turn_mla")[0:96, 0:96], A[0:96, j - 1, :], True, True, small_full)
            begin("mla_k")
            pe.wait_ge(S("mla_normed"), 5)
            for j in range(8):
                w = weight(2)
                for e in range(2):
                    m = product()
                    for k in range(2):
                        mm(pbank(m)[0:64, :], w[:, k * P + 64 * e:k * P + 64 * e + 64], B[:, 19 + k, :], k == 0, k == 1,
                           product_full if k == 1 else None)
            begin("mla_v")
            for half in range(2):
                token_major(lambda k: B[:, 19 + k, :], 2, T, settled)
            begin("mla")
            pe.wait_ge(S("mla_q_ready"), 16)
            pe.wait_ge(S("mla_keys_spread"), 1)
            for j in range(4):
                done(pe, AT["mla_k"][0] + 12 + j)
            for j in range(4):
                done(pe, AT["mla_v"][0] + 4 + j)
            for u in range(16 * NB + MLAG):
                if u < 16 * NB:
                    hd, n = u // NB, u % NB
                    s = small()
                    mm(sbank(s)[:, 0:(n + 1) * P], A[0:96, hd, n * P:(n + 1) * P], B[0:96, hd, 0:(n + 1) * P], True, True,
                       small_full)
                if u >= MLAG:
                    v = u - MLAG
                    hd, n = v // NB, v % NB
                    s = small()
                    pe.wait_ge(S("mla_probs"), v + 1)
                    for b in range(n + 1):
                        i = pe.transpose(sbank(s)[:, b * P:(b + 1) * P], TM[:, v % 4, b * P:(b + 1) * P], const("ident"))
                    i.then_inc(small_full, 1)
                    if n == NB - 1:
                        o = small()
                        for j in range(NB):
                            sdone(pe, mla_small("turned", v - 3 + j))
                        rows = slice(64 * (hd % 2), 64 * (hd % 2) + 64)
                        for b in range(NB):
                            mm(sbank(o)[rows, b * P:], A[:, 16 + 2 * b + hd // 8, hd % 8 * 64:hd % 8 * 64 + 64],
                               B[:, 16 + 4 * (hd % 2) + b, b * P:], b == 0, b == NB - 1,
                               small_full if b == NB - 1 else None)
            begin("mla_out")
            sdone(pe, mla_small("output", 14))
            sdone(pe, mla_small("output", 15))
            for j in range(DB):
                project(h, DB, settled)
            norm_sum(8)
            up(8, 3, 8)
            down(8, FF2)
            norm_sum(9)
            up(9, 3, 8)
            down(9, FF2)
            norm_sum(10)
            begin("rw_in")
            for n in range(6):
                xs = lambda k: B[:, 8 * (n % 2) + k, :]
                mixed = lambda k: pe.wait_ge(S("mixed"), DB * n + k + 1)
                for j in range((8, 8, 8, 1, 1, 2)[n]):
                    project(xs, DB, mixed if j == 0 else settled)
            m0 = AT["rw_in"][0] + 24
            for n in range(2):
                done(pe, m0 + n)
                for j in range(8):
                    project(lambda k: TM[:, n, :], 1, settled, rows=64)
            begin("rw_prep")
            for j in range(DB):
                s = small()
                pe.wait_ge(S("kk_square"), j + 1)
                mm(sbank(s)[:, :], const("halves"), SQ[:, j % 2, :], True, True, small_full)
                s = small()
                pe.wait_ge(S("bonus_product"), j + 1)
                mm(sbank(s)[:, :], const("halves"), TM[:, 3, :], True, True, small_full)
            begin("rw")
            def product_matrix(step, j):
                left, right = MATRICES[j // 2]
                s = small()
                rows = slice(64 * (j % 2), 64 * (j % 2) + 64)
                x = scaled_of[step % 2]
                for b in range(2):
                    mm(sbank(s)[:, b * P:(b + 1) * P], x[rows, left + b, :], x[rows, right + b, :],
                       True, True, small_full if b else None)

            pe.wait_ge(S("rw_scaled"), 2)
            for j in range(4):
                product_matrix(0, j)
            for i, (c, g) in enumerate(STEPS):
                scaled = scaled_of[i % 2]

                def matrix(j):
                    product_matrix(i, j)

                def turned(j):
                    s = small()
                    for b in range(2 if j else 4):
                        x = A[:, 16 + 2 * g + b, c * P:(c + 1) * P] if j else scaled[:, 4 + b, :]
                        t = pe.transpose(sbank(s)[:, b * P:(b + 1) * P], x, const("ident"))
                    t.then_inc(small_full, 1)

                def z(half):
                    s = small()
                    pe.wait_ge(S("rw_start"), i + 1)
                    sdone(pe, rw_small(i, "turned", 1))
                    sdone(pe, rw_small(i, "matrix", 4 + half))
                    rows = slice(64 * half, 64 * half + 64)
                    for b in range(2):
                        o = sbank(s)[:, 64 * b:64 * b + 64]
                        mm(o, scaled[rows, b, :], START[rows, b, :], True, False)
                        mm(o, RW[:, 2, (2 * half + b) * P:(2 * half + b + 1) * P], tok[:, 4 + b, 64 * half:64 * half + 64],
                           False, True, small_full if b else None)

                fill = {"matrix": matrix, "turned": turned, "z": z}
                pe.wait_ge(S("inverse_started"), 2 * (i + 1))
                for lv in range(6):
                    s = small()
                    if lv:
                        sdone(pe, rw_small(i, "inv", lv - 1))
                    for e in range(4):
                        q = slice(e * P, (e + 1) * P)
                        mm(sbank(s)[:, q], RW[:, 1, q], INV[:, q], True, True, small_full if e == 3 else None)
                    for what, j in FILL[lv]:
                        fill[what](j)
                    sdone(pe, s)
                    if lv:
                        sdone(pe, rw_small(i, "invt", lv - 1))
                    if lv < 5:
                        x = small()
                        for e in range(4):
                            q = slice(e * P, (e + 1) * P)
                            mm(sbank(x)[:, q], INVT[:, q], LOW[:, q], True, True, small_full if e == 3 else None)
                    x = small()
                    for e in range(4):
                        q = slice(e * P, (e + 1) * P)
                        mm(sbank(x)[:, q], LOW[:, q], INVT[:, q], True, True, small_full if e == 3 else None)
                if i + 1 < len(STEPS):
                    pe.wait_ge(S("rw_scaled"), 2 * (i + 2))
                    for j in range(4):
                        product_matrix(i + 1, j)
                s = small()
                sdone(pe, rw_small(i, "invt", 5))
                for half in range(2):
                    sdone(pe, rw_small(i, "z", half))
                for e in range(4):
                    mm(sbank(s)[:, 64 * e:64 * e + 64], INVT[:, e * P:(e + 1) * P], Z[:, e, :], True, True,
                       small_full if e == 3 else None)
                u = s
                for j in range(6, 10):
                    sdone(pe, rw_small(i, "matrix", j))
                for half in range(2):
                    s = small()
                    rows = slice(64 * half, 64 * half + 64)
                    for b in range(2):
                        e = 2 * half + b
                        o = sbank(s)[rows, b * P:(b + 1) * P]
                        mm(o, START[rows, b, :], scaled[rows, 2 + b, :], True, False)
                        mm(o, tok[:, 4 + b, 64 * half:64 * half + 64], RW[:, 4, e * P:(e + 1) * P], False, False)
                        sdone(pe, u)
                        mm(o, U[:, e, :], RW[:, 3, e * P:(e + 1) * P], False, True, small_full if b else None)
                sdone(pe, rw_small(i, "turned", 0))
                for half in range(2):
                    s = small()
                    rows = slice(64 * half, 64 * half + 64)
                    for b in range(2):
                        o = sbank(s)[rows, 64 * b:64 * b + 64]
                        mm(o, tok[:, b, rows], U[:, 2 * half + b, :], True, False)
                        mm(o, tok[:, 2 + b, rows], tok[:, 4 + b, rows], False, True, small_full if b else None)
            begin("rw_g")
            for half in range(2):
                for i in range(12, 16):
                    sdone(pe, rw_small(i, "y", half))
            for j in range(DB + 1):
                if j < DB:
                    s = small()
                    mm(sbank(s)[:, :], const("halves"), A[:, j, :], True, True, small_full)
                    m = product()
                    for k in range(2):
                        rows = P if k == 0 else LORA_G - P
                        mm(pbank(m)[:, :], weight()[0:rows, :], PT[0:rows, k, :], k == 0, k == 1,
                           product_full if k else None)
                if j >= 1:
                    s = small()
                    pe.wait_ge(S("gn_square"), j)
                    mm(sbank(s)[:, :], const("halves"), SQ[:, (j - 1) % 2, :], True, True, small_full)
            begin("rw_out")
            for j in range(DB):
                project(lambda k: B[:, k, :], DB,
                        (lambda k: done(pe, AT["rw_g"][0] + k)) if j == 0 else settled)
            norm_sum(11)
            up(11, 3, 8)
            down(11, FF2)
            norm_sum(12)
            begin("end")


        @block.scalar
        def _(act):
            count = {"n": 0}

            def a(out, in_, func, **kw):
                return act.activation(out, in_, func, **kw)

            def own(i):
                count["n"] += 1
                i.then_inc(S("scalar_step"), 1)
                act.wait_ge(S("scalar_step"), count["n"])

            def took(i, m):
                i.then_inc(product_done[m % 4], 1)

            def stook(i, s):
                i.then_inc(small_done[s % 4], 1)

            def norm(n):
                s = AT[f"norm{n}"][1]
                for k in range(DB):
                    if n:
                        done(act, update(n, k))
                    if k >= 2:
                        act.wait_ge(S("square_used"), (DB - 1) * n + k - 1)
                    a(SQ[:, k % 2, :], X[:, k, :], ACT.Square).then_inc(S("square_ready"), 1)
                sfull(act, s)
                stook(a(RB[:, :], sbank(s)[:, :], ACT.Sqrt, scale=1 / 1024, bias=vec("eps", 0)), s)

            def up_conv(n, layer):
                m0 = AT[f"up{n}"][0]
                w = lambda j: V[:, j + (VAT["ff_conv_w"] + layer * 3 * FF1 + 2 * FF1), :]
                b = lambda j: V[:, j + (VAT["ff_conv_b"] + layer * FF1), :]
                with act.Fori(0, 4) as i:
                    for j in range(6):
                        m = up_product(n, 2 * j)
                        full(act, m, i * 16)
                        done(act, up_product(n, 2 * j - 3), i * 4)
                        a(TM[:, j % 2, :], pbank(m)[:, :], ACT.Identity, scale=w(i * 6 + j),
                          bias=b(i * 6 + j)).then_inc(S("tap_ready"), 1)
                        done(act, m, i * 4)
                        a(TM[:, 2 + j % 2, :], TM[:, j % 2, :], ACT.Gelu_apprx_tanh).then_inc(S("gelu_ready"), 1)

            def ple(n):
                m0 = AT[f"ple{n}"][0]
                for j in range(DB):
                    m = m0 + 2 * j
                    full(act, m)
                    if j >= 2:
                        done(act, m - 3)
                    took(a(TM[:, j % 2, :], pbank(m)[:, :], ACT.Sigmoid), m)

            act.wait_ge(S("x_landed"), 16)
            act.wait_ge(S("vectors_landed"), 16)
            a(SM[:, 80:88], V[:, VAT["c"]:VAT["c"] + 8, 0], ACT.Silu).then_inc(S("c_act"), 1)
            norm(0)
            lam = V[:, VAT["rg_lambda"]:VAT["rg_lambda"] + 4, 0]
            own(a(SM[:, 0:4], lam, ACT.Abs))
            own(a(SM[:, 4:8], SM[:, 0:4], ACT.Exp, scale=-1.0))
            act.wait_ge(S("lambda_one_plus"), 1)
            a(SM[:, 12:16], SM[:, 8:12], ACT.Ln).then_inc(S("lambda_log"), 1)
            m0 = AT["hy_in"][0]
            for j in range(12):
                full(act, m0 + j)
                if j >= 4:
                    act.wait_ge(S("conv_done"), j - 3)
                took(a(TM[:, j, :] if j < 4 else TM[:, j % 4, :], pbank(m0 + j)[:, :], ACT.Identity,
                       bias=vec("hy_b", (j if j < 4 else j + 4))), m0 + j)
            for j in range(4):
                m = m0 + 12 + j
                full(act, m)
                took(a(A[:, 12 + j, :], pbank(m)[:, :], ACT.Gelu_apprx_tanh, bias=vec("hy_b", 4 + j)), m)
            for j in range(4):
                m = m0 + 16 + j
                full(act, m)
                took(a(A[:, 8 + j, :], pbank(m)[:, :], ACT.Sigmoid, bias=vec("hy_b", 20 + j)), m)
            for j in range(2):
                m = m0 + 20 + j
                full(act, m)
                took(a(A[0:4, 20 + j, :], pbank(m)[0:4, :], ACT.Identity, bias=V[0:4, VAT["hy_b"] + 24 + j, :]), m)
            s0 = AT["rg"][1]
            for j in range(4):
                for g, name in enumerate(("rg_b_a", "rg_b_x")):
                    s = s0 + 2 * j + g
                    sfull(act, s)
                    stook(a(B[:, 8 + 4 * g + j, :], sbank(s)[:, :], ACT.Sigmoid, bias=vec(name, j)), s)
            act.wait_ge(S("conv_done"), 12)
            a(A[:, 0:8, :], A[:, 0:8, :], ACT.Silu).then_inc(S("qk_ready"), 1)
            done(act, m0 + 21)
            own(a(A[0:4, 22, :], A[0:4, 21, :], ACT.Abs))
            own(a(A[0:4, 22, :], A[0:4, 22, :], ACT.Exp, scale=-1.0))
            a(A[0:4, 22, :], A[0:4, 22, :], ACT.Ln, bias=1.0).then_inc(S("f_log"), 1)
            act.wait_ge(S("log_a"), 4)
            a(B[:, 0:4, :], B[:, 8:12, :], ACT.Exp, scale=-1.0).then_inc(S("rg_a"), 1)
            a(B[:, 16:20, :], B[:, 8:12, :], ACT.Tanh).then_inc(S("rg_tanh"), 1)
            act.wait_ge(S("rg_ratio"), 1)
            a(B[:, 16:20, :], B[:, 16:20, :], ACT.Sqrt, scale=2.0).then_inc(S("rg_root"), 1)
            s0 = AT["ml"][1]
            act.wait_ge(S("y_rg"), 1)
            for j in range(8):
                s = s0 + 1 + j
                sfull(act, s)
                if j < 4:
                    stook(a(B[:, 4 + j, :], sbank(s)[:, :], ACT.Identity), s)
                else:
                    stook(a(B[:, 4 + j, :], sbank(s)[:, :], ACT.Exp, scale=-1.0), s)
            for hd in range(4):
                for j in range(NB):
                    w = B[:, 12 + 4 * (hd % 2) + j, j * P:]
                    act.wait_ge(S("ml_exponent"), 4 * hd + j + 1)
                    a(w, w, ACT.Exp).then_inc(S("ml_exp"), 1)
                den = s0 + 9 + 7 * hd + 5
                sfull(act, den)
                stook(a(TM[:, 0, :], sbank(den)[:, :], ACT.Abs), den)
                sdone(act, den - 1)
                a(SQ[:, 0, :], A[:, hd, :], ACT.Square).then_inc(S("ml_square"), 1)
                sfull(act, den + 1)
                stook(a(TM[:, 1, :], sbank(den + 1)[:, :], ACT.Sqrt, scale=1 / 128, bias=vec("eps", 0)), den + 1)
            norm(1)
            up_conv(1, 0)
            norm(2)
            ple(2)
            norm(3)
            m0 = AT["at_in"][0]
            act.wait_ge(S("angles"), 1)
            own(a(B[:, 0, :], B[:, 0, :], ACT.Sin))
            own(a(B[:, 1, :], B[:, 1, :], ACT.Sin))
            a(B[:, 1, :], B[:, 1, :], ACT.Square).then_inc(S("sines"), 1)
            for j in range(12):
                full(act, m0 + j)
                if j >= 2:
                    act.wait_ge(S("at_scaled"), j - 1)
                took(a(TM[:, j % 2, :], pbank(m0 + j)[:, :], ACT.Identity), m0 + j)
                done(act, m0 + j)
                a(SQ[:, j % 2, :], TM[:, j % 2, :], ACT.Square).then_inc(S("at_square"), 1)
                s = at_in_small("sum", j)
                sfull(act, s)
                if j >= 1:
                    act.wait_ge(S("at_scaled"), j)
                stook(a(RB[:, :], sbank(s)[:, :], ACT.Sqrt, scale=1 / 64, bias=vec("eps", 0)), s)
            for u in range(32 + LAG):
                if u < 32:
                    act.wait_ge(S("at_minus_max"), u + 1)
                    n, g, half = u // 8, u // 2 % 4, u % 2
                    for e in range(2):
                        o = 2 * (u % 4) + e
                        p = TM[:, u % 4, 256 * e + (0 if n else 128):256 * e + 256]
                        a(p, p, ACT.Exp, bias=SM[:, o:o + 1], accum_out=SM[:, 8 + o:9 + o]).then_inc(S("at_exp"), 1)
                        a(SM[:, 16 + o:17 + o], vec("at_sinks", 4 * g + 2 * e + half), ACT.Exp,
                          bias=SM[:, o:o + 1]).then_inc(S("at_exp"), 1)
                if 0 <= u - LAG + 1 < 32:
                    v = u - LAG + 1
                    s = at_small("turned", v)
                    sfull(act, s)
                    for e in range(2):
                        cols = slice(256 * e + (0 if v >= 8 else 128), 256 * e + 256)
                        i = a(B[:, 12 + v % 4, cols], sbank(s)[:, cols], ACT.Identity)
                    stook(i, s)
                if u >= LAG:
                    v = u - LAG
                    n, g, half = v // 8, v // 2 % 4, v % 2
                    s = at_small("output", v)
                    sfull(act, s)
                    rows = slice(64 * half, 64 * half + 64)
                    stook(a(B[rows, 4 + 2 * g:6 + 2 * g, n * P:(n + 1) * P],
                            sbank(s)[rows, 0:256].rearrange("p (e t) -> p e t", e=2), ACT.Identity), s)
            norm(4)
            up_conv(4, 1)
            norm(5)
            ple(5)
            def up_silu(n):
                m0 = AT[f"up{n}"][0]

                def pair(m, j, i, rounds):
                    full(act, m, i)
                    done(act, m - 3, rounds)
                    took(a(TM[:, j % 2, :], pbank(m)[:, :], ACT.Silu), m)
                with act.Fori(0, 3) as i:
                    for j in range(6):
                        pair(m0 + 2 * j, j, i * 12, i * 3)
                for j in range(18, FF2):
                    pair(m0 + 2 * j, j, 0, 0)

            norm(6)
            up_silu(6)
            norm(7)
            m0, s0 = AT["mla_in"][:2]
            for j in range(6):
                full(act, m0 + j)
                took(a(B[:, 16 + j, :], pbank(m0 + j)[:, :], ACT.Identity), m0 + j)
            for j in range(5):
                if j in (2, 3):
                    act.wait_ge(S("mla_square_used"), j - 1)
                if j == 4:
                    sfull(act, s0)
                done(act, m0 + j)
                a(SQ[:, j % 2, :], B[:, 16 + j, :], ACT.Square).then_inc(S("mla_square"), 1)
            for j, width in ((0, 384), (1, 256)):
                sfull(act, s0 + j)
                stook(a(TM[:, j, :], sbank(s0 + j)[:, :], ACT.Sqrt, scale=1 / width, bias=vec("eps", 0)), s0 + j)
            m0 = AT["mla_q"][0]
            for j in range(16):
                full(act, m0 + j)
                took(a(A[0:96, j, :], pbank(m0 + j)[0:96, :], ACT.Identity), m0 + j)
            m0 = AT["mla_k"][0]
            for j in range(16):
                full(act, m0 + j)
                took(a(B[0:64, j, :], pbank(m0 + j)[0:64, :], ACT.Identity), m0 + j)
            for u in range(16 * NB + MLAG - 1):
                if u < 16 * NB:
                    n, o = u % NB, u % 4
                    act.wait_ge(S("mla_minus_max"), u + 1)
                    p = TM[:, o, 0:(n + 1) * P]
                    a(p, p, ACT.Exp, bias=SM[:, o:o + 1], accum_out=SM[:, 4 + o:5 + o]).then_inc(S("mla_exp"), 1)
                if u < MLAG - 1:
                    continue
                v = u - MLAG + 1
                hd, n = v // NB, v % NB
                s = mla_small("turned", v)
                sfull(act, s)
                if v >= 8 and n == 0:
                    sfull(act, mla_small("output", hd - 2))
                stook(a(B[:, 16 + 4 * (hd % 2):17 + 4 * (hd % 2) + n, n * P:(n + 1) * P],
                        sbank(s)[:, 0:(n + 1) * P].rearrange("p (b t) -> p b t", t=P), ACT.Identity), s)
                if n == NB - 1:
                    s = mla_small("output", hd)
                    rows = slice(64 * (hd % 2), 64 * (hd % 2) + 64)
                    sfull(act, s)
                    stook(a(H[rows, hd // 2, :], sbank(s)[rows, :], ACT.Identity), s)
            norm(8)
            up_silu(8)
            norm(9)
            up_silu(9)
            norm(10)
            m0 = AT["rw_in"][0]
            for j in range(24):
                full(act, m0 + j)
                took(a(A[:, j, :], pbank(m0 + j)[:, :], ACT.Identity), m0 + j)
            for j, (out, rows, func) in enumerate(((TM[0:64, 0, :], 64, ACT.Tanh), (TM[0:64, 1, :], 64, ACT.Identity),
                                                   (PT[:, 0, :], P, ACT.Sigmoid), (PT[0:32, 1, :], 32, ACT.Sigmoid))):
                m = m0 + 24 + j
                full(act, m)
                took(a(out, pbank(m)[0:rows, :], func), m)
            for n, (first, name) in enumerate(((16, "rwkv_w0"), (8, "rwkv_a0"))):
                for j in range(DB):
                    m = m0 + 28 + 8 * n + j
                    full(act, m)
                    took(a(B[:, first + j, :], pbank(m)[:, :], ACT.Sigmoid, bias=vec(name, j)), m)
            s0 = AT["rw_prep"][1]
            for j in range(DB):
                act.wait_ge(S("kk_raw"), j + 1)
                if j >= 2:
                    sfull(act, s0 + 2 * (j - 2))
                a(SQ[:, j % 2, :], B[:, j, :], ACT.Square).then_inc(S("kk_square"), 1)
                sdone(act, s0 + 2 * j)
                a(TM[:, j % 2, :], TM[:, j % 2, :], ACT.Sqrt).then_inc(S("kk_root"), 1)
            def decays(i):
                c, g = STEPS[i]
                act.wait_ge(S("rw_middle"), i + 1)
                for b in range(2):
                    d = B[:, 16 + 2 * g + b, c * P:(c + 1) * P]
                    a(GROW[:, b, 0:1], DV[:, b:b + 1], ACT.Exp)
                    a(GROW[:, b, 1:129], d, ACT.Exp, scale=-DECAY, bias=DV[:, b:b + 1])
                    a(SHRINK[:, b, :], d, ACT.Exp, scale=DECAY, bias=DN[:, b:b + 1])
                a(DS[i % 2], DN, ACT.Exp).then_inc(S("rw_decays"), 1)

            decays(0)
            for i, (c, g) in enumerate(STEPS):
                if i + 1 < len(STEPS):
                    decays(i + 1)
                s = rw_small(i, "turned", 1)
                sfull(act, s)
                stook(a(TM[:, 3, 0:256], sbank(s)[:, 0:256], ACT.Identity), s)
                s = rw_small(i, "turned", 0)
                sfull(act, s)
                stook(a(TM[:, 2, :], sbank(s)[:, :], ACT.Identity), s)
                for half in range(2):
                    s = rw_small(i, "z", half)
                    sfull(act, s)
                    stook(a(Z[:, 2 * half:2 * half + 2, :], sbank(s)[:, 0:P].rearrange("p (b v) -> p b v", v=64),
                            ACT.Identity), s)
                for half in range(2):
                    s = rw_small(i, "y", half)
                    rows = slice(64 * half, 64 * half + 64)
                    sfull(act, s)
                    stook(a(A[rows, 2 * g:2 * g + 2, c * P:(c + 1) * P],
                            sbank(s)[rows, 0:256].rearrange("p (b t) -> p b t", t=P), ACT.Identity), s)
            for j in range(DB + 1):
                if j < DB:
                    act.wait_ge(S("gn_centred"), j + 1)
                    a(SQ[:, j % 2, :], TM[:, j % 2, :], ACT.Square).then_inc(S("gn_square"), 1)
                if j >= 1:
                    s = gn_small("variance", j - 1)
                    sfull(act, s)
                    stook(a(TM[:, 2 + (j - 1) % 2, :], sbank(s)[:, :], ACT.Sqrt, scale=1 / 64, bias=vec("gn_eps", 0)), s)
            norm(11)
            up_silu(11)
            norm(12)

        @block.vector
        def _(dve):
            count = {"n": 0}
            mods3 = MODS[:, :, 0].rearrange("p (q j) -> p q j", j=3)
            bias3 = V[:, VAT["ada_b"]:VAT["ada_b"] + 144, 0].rearrange("p (q j) -> p q j", j=3)
            ts, tt, stt = dve.tensor_scalar, dve.tensor_tensor, dve.scalar_tensor_tensor

            def own(i):
                count["n"] += 1
                i.then_inc(S("vector_step"), 1)
                dve.wait_ge(S("vector_step"), count["n"])

            def took(i, m):
                i.then_inc(product_done[m % 4], 1)

            def stook(i, s):
                i.then_inc(small_done[s % 4], 1)

            def norm(n, gain, shift=None, out=None):
                sdone(dve, AT[f"norm{n}"][1])
                own(dve.reciprocal(RB[:, :], RB[:, :]))
                for k in range(DB):
                    i = stt(H[:, k, :], X[:, k, :], gain(k), RB[:, :], ALU.mult, ALU.mult)
                    if shift is not None:
                        own(i)
                        i = ts(H[:, k, :], H[:, k, :], shift(k), None, ALU.add)
                    i.then_inc(out or S("normed_ready"), 1)

            def up_conv(n, layer):
                w = lambda tap, j: V[:, j + (VAT["ff_conv_w"] + layer * 3 * FF1 + tap * FF1), :]
                base = count["n"]
                taps = 24 * layer
                with dve.Fori(0, 4) as i:
                    for j in range(6):
                        m, mu = up_product(n, 2 * j), up_product(n, 2 * j + 1)
                        t = TM[:, j % 2, :]
                        dve.wait_ge(S("tap_ready"), i * 6 + (taps + j + 1))
                        stt(t[:, 1:], pbank(m)[:, 0:T - 1], w(1, i * 6 + j), t[:, 1:], ALU.mult, ALU.add)\
                            .then_inc(S("vector_step"), 1)
                        dve.wait_ge(S("vector_step"), i * 6 + (base + j + 1))
                        took(stt(t[:, 2:], pbank(m)[:, 0:T - 2], w(0, i * 6 + j), t[:, 2:], ALU.mult, ALU.add), m)
                        dve.wait_ge(S("gelu_ready"), i * 6 + (taps + j + 1))
                        full(dve, mu, i * 16)
                        took(tt(A[:, i * 6 + j, :], TM[:, 2 + j % 2, :], pbank(mu)[:, :], ALU.mult), mu)
                        for q in range(4):
                            if up_product(n, 3 * q + 2) in (m, mu):
                                columns(up_product(n, 3 * q + 2) + 1, i * 4 + (24 * layer + q), i * 16)
                count["n"] = base + 24

            def columns(m, at, more=0):
                full(dve, m, more)
                took(tt(mods3[:, at, :], pbank(m)[:, 0:3], bias3[:, at, :], ALU.add), m)

            def add(name):
                m0 = AT[name][0]
                step = 2 if name.startswith("down") else 1
                for k in range(DB):
                    m = m0 + step * k
                    full(dve, m)
                    took(tt(X[:, k, :], X[:, k, :], pbank(m)[:, :], ALU.add), m)
                    if step == 2:
                        columns(m + 1, (16 if name == "down1" else 40) + k)

            def ple(n):
                m0 = AT[f"ple{n}"][0]
                for j in range(DB):
                    m = m0 + 2 * j
                    done(dve, m)
                    full(dve, m + 1)
                    own(tt(TM[:, 2 + j % 2, :], TM[:, j % 2, :], pbank(m + 1)[:, :], ALU.mult))
                    took(tt(X[:, j, :], X[:, j, :], TM[:, 2 + j % 2, :], ALU.add), m + 1)

            dve.wait_ge(S("vectors_landed"), 16)
            dve.wait_ge(S("x_landed"), 16)
            norm(0, lambda k: vec("norm_mix", k))
            dve.wait_ge(S("scalar_step"), 2)
            e, u, lg = SM[:, 4:8], SM[:, 8:12], SM[:, 12:16]
            ts(u, e, 1.0, None, ALU.add).then_inc(S("lambda_one_plus"), 1)
            dve.wait_ge(S("lambda_one_plus"), 1)
            own(ts(SM[:, 16:20], u, -1.0, None, ALU.add))
            own(ts(SM[:, 20:24], SM[:, 16:20], 0.0, None, ALU.is_equal))
            own(tt(SM[:, 16:20], SM[:, 16:20], SM[:, 20:24], ALU.add))
            own(dve.reciprocal(SM[:, 16:20], SM[:, 16:20]))
            dve.wait_ge(S("lambda_log"), 1)
            own(tt(lg, lg, SM[:, 20:24], ALU.add))
            own(tt(lg, lg, SM[:, 16:20], ALU.mult))
            own(tt(lg, lg, e, ALU.mult))
            lam = V[:, VAT["rg_lambda"]:VAT["rg_lambda"] + 4, 0]
            own(ts(SM[:, 24:28], lam, -1.0, 0.0, ALU.mult, ALU.max))
            own(tt(lg, lg, SM[:, 24:28], ALU.add))
            own(ts(lg, lg, RG_C, None, ALU.mult))
            m0 = AT["hy_in"][0]
            for j in range(12):
                raw = TM[:, j % 4, :]
                out = B[:, 4 + j, :] if j < 4 else A[:, j - 4, :]
                w = (lambda tap: vec("rg_conv_w", 4 * tap + j)) if j < 4 else (lambda tap: vec("ml_conv_w", 8 * tap + j - 4))
                b = vec("rg_conv_b", j) if j < 4 else vec("ml_conv_b", j - 4)
                done(dve, m0 + j)
                own(ts(out, raw, w(3), b, ALU.mult, ALU.add))
                own(stt(out[:, 1:], raw[:, 0:T - 1], w(2), out[:, 1:], ALU.mult, ALU.add))
                own(stt(out[:, 2:], raw[:, 0:T - 2], w(1), out[:, 2:], ALU.mult, ALU.add))
                stt(out[:, 3:], raw[:, 0:T - 3], w(0), out[:, 3:], ALU.mult, ALU.add).then_inc(S("conv_done"), 1)
            dve.wait_ge(S("v_bias_landed"), 16)
            for t in range(NB):
                m = m0 + 22 + t
                full(dve, m)
                took(tt(A[:, 16 + t, :], pbank(m)[:, :], RW[:, 0, :], ALU.add), m)
            s0 = AT["rg"][1]
            for j in range(4):
                sdone(dve, s0 + 2 * j)
                ts(B[:, 8 + j, :], B[:, 8 + j, :], SM[:, 12 + j:13 + j], None, ALU.mult).then_inc(S("log_a"), 1)
            i_, f, g, ones = A[0:4, 20, :], A[0:4, 21, :], A[0:4, 22, :], A[0:4, 23, :]
            own(dve.memset(ones, 1.0))
            dve.wait_ge(S("f_log"), 1)
            own(stt(f, f, 0.0, g, ALU.min, ALU.subtract))
            own(dve.tensor_tensor_scan(g, ones, f, 0.0, ALU.mult, ALU.add))
            done(dve, m0 + 20)
            own(tt(i_, i_, g, ALU.subtract))
            own(dve.tensor_tensor_scan(f, i_, i_, -3.0e38, ALU.max, ALU.max))
            tt(g, g, f, ALU.add).then_inc(S("gate_rows"), 1)
            ts(ones, f, -1.0, None, ALU.mult).then_inc(S("gate_rows"), 1)
            dve.wait_ge(S("rg_a"), 1)
            dve.wait_ge(S("rg_tanh"), 1)
            own(ts(B[:, 8:12, :], B[:, 16:20, :], 1.0, None, ALU.add))
            own(dve.reciprocal(B[:, 8:12, :], B[:, 8:12, :]))
            own(tt(B[:, 16:20, :], B[:, 16:20, :], B[:, 8:12, :], ALU.mult))
            ts(B[:, 16:20, :], B[:, 16:20, :], 1e-33, None, ALU.max).then_inc(S("rg_ratio"), 1)
            for j in range(4):
                sdone(dve, s0 + 2 * j + 1)
            own(tt(B[:, 12:16, :], B[:, 12:16, :], B[:, 4:8, :], ALU.mult))
            dve.wait_ge(S("rg_root"), 1)
            own(tt(B[:, 16:20, :], B[:, 16:20, :], B[:, 12:16, :], ALU.mult))
            for j in range(4):
                own(dve.tensor_tensor_scan(B[:, 8 + j, :], B[:, j, :], B[:, 16 + j, :], 0.0, ALU.mult, ALU.add))
            for j in range(4):
                done(dve, m0 + 12 + j)
            tt(B[:, 20:24, :], B[:, 8:12, :], A[:, 12:16, :], ALU.mult).then_inc(S("y_rg"), 1)
            s0 = AT["ml"][1]
            sfull(dve, s0)
            dve.tensor_copy(SM[:, 32:48], sbank(s0)[:, 0:16]).then_inc(small_done[s0 % 4], 1)
            sdone(dve, s0)
            for hd in range(4):
                sdone(dve, s0 + 1 + hd)
                first = s0 + 9 + 7 * hd
                for j in range(NB):
                    a_s = SM[:, 32 + 4 * j + hd:33 + 4 * j + hd]
                    if hd >= 2 and j == 0:
                        sfull(dve, first - 14 + 5)
                    ts(B[:, 12 + 4 * (hd % 2) + j, j * P:], B[:, 4 + hd, j * P:], a_s, 0.0, ALU.add, ALU.min)\
                        .then_inc(S("ml_exponent"), 1)
                for j in range(NB):
                    s = first + j
                    w = B[:, 12 + 4 * (hd % 2) + j, j * P:]
                    dve.wait_ge(S("ml_masked"), 4 * hd + j + 1)
                    sfull(dve, s)
                    stook(stt(w, sbank(s)[:, j * P:], float(128 ** -0.5), w, ALU.mult, ALU.mult), s)
                num, den = first + 4, first + 5
                sdone(dve, den)
                sdone(dve, s0 + 5 + hd)
                own(tt(TM[:, 0, :], TM[:, 0, :], B[:, 8 + hd, :], ALU.max))
                own(dve.reciprocal(TM[:, 0, :], TM[:, 0, :]))
                sfull(dve, num)
                stook(tt(A[:, hd, :], sbank(num)[:, :], TM[:, 0, :], ALU.mult), num)
                sdone(dve, den + 1)
                own(dve.reciprocal(TM[:, 1, :], TM[:, 1, :]))
                own(stt(TM[:, 2, :], A[:, hd, :], vec("ml_norm", hd), TM[:, 1, :], ALU.mult, ALU.mult))
                done(dve, m0 + 16 + hd)
                tt(B[:, hd, :], TM[:, 2, :], A[:, 8 + hd, :], ALU.mult).then_inc(S("y_ml"), 1)
            add("hy_out")
            norm(1, lambda k: vec("norm_ffn", k))
            up_conv(1, 0)
            add("down1")
            norm(2, lambda k: vec("norm_ple", k))
            ple(2)
            dve.wait_ge(S("positions_landed"), 16)
            own(dve.tensor_copy(B[:, 0, :], B[:, 2, :].bitcast(I32)))
            own(ts(B[:, 0, :], B[:, 0, :], vec("inv_freq", 0), None, ALU.mult))
            own(ts(B[:, 1, :], B[:, 0, :], float(np.float32(0.5 / np.pi)), 12582912.0, ALU.mult, ALU.add))
            own(ts(B[:, 1, :], B[:, 1, :], -12582912.0, None, ALU.add))
            rest = 2 * np.pi
            for part in range(3):
                c = np.float32(rest) if part == 2 else np.float32(np.frexp(rest)[0] * 2 ** 9 // 1 / 2 ** 9 * 2.0 ** np.frexp(rest)[1])
                rest = rest - float(c)
                own(stt(B[:, 0, :], B[:, 1, :], -float(c), B[:, 0, :], ALU.mult, ALU.add))
            own(ts(B[:, 0, :], B[:, 0, :], 3.1415925, -3.1415925, ALU.min, ALU.max))
            ts(B[:, 1, :], B[:, 0, :], 0.5, None, ALU.mult).then_inc(S("angles"), 1)
            norm(3, lambda k: vec("norm_mix", 8 + k))
            dve.wait_ge(S("sines"), 1)
            own(ts(B[:, 1, :], B[:, 1, :], -2.0, 1.0, ALU.mult, ALU.add))
            m0 = AT["at_in"][0]
            for j in range(12 + 1):
                if j < 12:
                    s = at_in_small("sum", j)
                    sdone(dve, s)
                    own(dve.reciprocal(RB[:, :], RB[:, :]))
                    stt(A[:, j, :], TM[:, j % 2, :], vec("at_q_norm" if j < 8 else "at_k_norm", 0), RB[:, :],
                        ALU.mult, ALU.mult).then_inc(S("at_scaled"), 1)
                if j >= 1:
                    b = j - 1
                    s = at_in_small("turned", b)
                    sfull(dve, s)
                    stook(tt(TM[:, 2 + b % 2, :], sbank(s)[:, :], B[:, 0, :], ALU.mult), s)
                    own(tt(A[:, b, :], A[:, b, :], B[:, 1, :], ALU.mult))
                    sdone(dve, s)
                    tt(A[:, b, :], A[:, b, :], TM[:, 2 + b % 2, :], ALU.add).then_inc(S("at_rotated"), 1)
            for t in range(NB):
                m = m0 + 12 + t
                full(dve, m)
                took(dve.tensor_copy(A[:, 12 + t // 2, t % 2 * 256:t % 2 * 256 + 256], pbank(m)[:, 0:256]), m)

            def at_scale(v):
                n = v // 8
                o = 2 * (v % 4)
                dve.wait_ge(S("at_exp"), 4 * v + 4)
                own(tt(SM[:, 24 + o:26 + o], SM[:, 8 + o:10 + o], SM[:, 16 + o:18 + o], ALU.add))
                own(dve.reciprocal(SM[:, 24 + o:26 + o], SM[:, 24 + o:26 + o]))
                lo = 0 if n else P
                own(ts(TM[:, v % 4, lo:256], TM[:, v % 4, lo:256], SM[:, 24 + o:25 + o], None, ALU.mult))
                ts(TM[:, v % 4, 256 + lo:512], TM[:, v % 4, 256 + lo:512], SM[:, 25 + o:26 + o], None, ALU.mult)\
                    .then_inc(S("at_probs"), 1)

            for u in range(32 + 1):
                if u < 32:
                    n, g, half = u // 8, u // 2 % 4, u % 2
                    o = 2 * (u % 4)
                    lo = 0 if n else P
                    s = at_small("scores", u)
                    sfull(dve, s)
                    if u >= 4:
                        sfull(dve, at_small("turned", u - 4))
                    w = TM[:, u % 4, :].rearrange("p (e k) -> p e k", e=2)[:, :, lo:256]
                    band = C[:, CAT["band"] + lo:CAT["band"] + 256]
                    for e in range(2):
                        i = stt(w[:, e, :], sbank(s)[:, 256 * e + lo:256 * e + 256], 0.125, band, ALU.mult, ALU.add)
                        if e == 1:
                            stook(i, s)
                    sdone(dve, s)
                    own(dve.tensor_reduce(SM[:, o:o + 2], w, AX, ALU.max))
                    for e in range(2):
                        h = 4 * g + 2 * e + half
                        i = ts(SM[:, o + e:o + e + 1], SM[:, o + e:o + e + 1], vec("at_sinks", h), -1.0, ALU.max, ALU.mult)
                    i.then_inc(S("at_minus_max"), 1)
                if u >= 1:
                    at_scale(u - 1)
            add("at_out")
            norm(4, lambda k: vec("norm_ffn", 8 + k))
            up_conv(4, 1)
            add("down4")
            norm(5, lambda k: vec("norm_ple", 8 + k))
            ple(5)
            mods = MODS[:, :, 0].rearrange("p (s w k) -> p s w k", w=3, k=8)
            gains = V[:, VAT["norm_g"]:VAT["norm_g"] + 48, 0].rearrange("p (s k) -> p s k", k=8)
            own(stt(GS[:, :, 0].rearrange("p (s k) -> p s k", k=8), mods[:, :, 1, :], 1.0, gains, ALU.add, ALU.mult))
            for sub in (0, 2, 3, 5):
                own(ts(mods[:, sub, 2, :], mods[:, sub, 2, :], 0.5, None, ALU.mult))

            def norm2(n, sub):
                norm(n, lambda k: GS[:, 8 * sub + k, :], lambda k: MODS[:, 24 * sub + k, :])

            def up_silu(n):
                m0 = AT[f"up{n}"][0]

                def pair(m, j, out, i, rounds):
                    done(dve, m, rounds)
                    full(dve, m + 1, i)
                    took(tt(out, TM[:, j % 2, :], pbank(m + 1)[:, :], ALU.mult), m + 1)
                with dve.Fori(0, 3) as i:
                    for j in range(6):
                        pair(m0 + 2 * j, j, A[:, i * 6 + j, :], i * 12, i * 3)
                for j in range(18, FF2):
                    pair(m0 + 2 * j, j, A[:, j, :], 0, 0)

            def add_gated(name, sub):
                m0 = AT[name][0]
                for k in range(DB):
                    full(dve, m0 + k)
                    took(stt(X[:, k, :], pbank(m0 + k)[:, :], MODS[:, 24 * sub + 16 + k, :], X[:, k, :], ALU.mult, ALU.add),
                         m0 + k)

            norm2(6, 0)
            up_silu(6)
            add_gated("down6", 0)
            norm2(7, 1)
            m0, s0 = AT["mla_in"][:2]
            for j0, n, name in ((0, 3, "mla_q_norm"), (3, 2, "mla_kv_norm")):
                t = TM[:, j0 // 3, :]
                sdone(dve, s0 + j0 // 3)
                own(dve.reciprocal(t, t))
                for j in range(n):
                    b = B[:, 16 + j0 + j, :]
                    stt(b, b, vec(name, j), t, ALU.mult, ALU.mult).then_inc(S("mla_normed"), 1)
            dve.wait_ge(S("mla_tables_landed"), 16)
            cos, sin = B[64:96, 22, :], B[64:96, 23, :]
            kr = B[64:96, 21, :]
            sfull(dve, s0 + 2)
            stook(tt(TM[64:96, 2, :], sbank(s0 + 2)[64:96, :], sin, ALU.mult), s0 + 2)
            own(tt(kr, kr, cos, ALU.mult))
            sdone(dve, s0 + 2)
            tt(kr, kr, TM[64:96, 2, :], ALU.add).then_inc(S("mla_key"), 1)
            s0 = AT["mla_q"][1]
            for j in range(16):
                q, t = A[64:96, j, :], TM[64:96, 2 + j % 2, :]
                sfull(dve, s0 + j)
                if j == 0:
                    dve.wait_ge(S("mla_key"), 1)
                stook(tt(t, sbank(s0 + j)[64:96, :], sin, ALU.mult), s0 + j)
                own(tt(q, q, cos, ALU.mult))
                sdone(dve, s0 + j)
                tt(q, q, t, ALU.add).then_inc(S("mla_q_ready"), 1)
            m0 = AT["mla_v"][0]
            for half in range(2):
                for t in range(NB):
                    m = m0 + 4 * half + t
                    full(dve, m)
                    took(dve.tensor_copy(A[:, 16 + 2 * t + half, :], pbank(m)[:, :]), m)
            scale = float(96 ** -0.5)
            for u in range(16 * NB + 1):
                if u < 16 * NB:
                    n, o = u % NB, u % 4
                    s, w = mla_small("scores", u), TM[:, o, 0:(n + 1) * P]
                    sfull(dve, s)
                    if u >= 4:
                        sfull(dve, mla_small("turned", u - 4))
                    stook(stt(w, sbank(s)[:, 0:(n + 1) * P], scale, C[:, CAT["causal"] + 512 - (n + 1) * P:CAT["causal"] + 512],
                              ALU.mult, ALU.add), s)
                    sdone(dve, s)
                    own(dve.tensor_reduce(SM[:, o:o + 1], w, AX, ALU.max))
                    ts(SM[:, o:o + 1], SM[:, o:o + 1], -1.0, None, ALU.mult).then_inc(S("mla_minus_max"), 1)
                if u >= 1:
                    v = u - 1
                    n, o = v % NB, v % 4
                    w = TM[:, o, 0:(n + 1) * P]
                    dve.wait_ge(S("mla_exp"), v + 1)
                    own(dve.reciprocal(SM[:, 8 + o:9 + o], SM[:, 4 + o:5 + o]))
                    ts(w, w, SM[:, 8 + o:9 + o], None, ALU.mult).then_inc(S("mla_probs"), 1)
            add_gated("mla_out", 1)
            norm2(8, 2)
            up_silu(8)
            add_gated("down8", 2)
            norm2(9, 3)
            up_silu(9)
            add_gated("down9", 3)
            norm2(10, 4)
            m0 = AT["rw_in"][0]
            mu = V[:, VAT["rwkv_mu"]:VAT["rwkv_mu"] + 48, 0]
            own(ts(SM[:, 0:48], mu, -1.0, 1.0, ALU.mult, ALU.add))
            last = (7, 15, 23, 24, 25, 27)
            dve.wait_ge(S("normed_ready"), DB * 11)
            for n in range(6):
                if n >= 2:
                    full(dve, m0 + last[n - 2])
                for k in range(DB):
                    b = B[:, 8 * (n % 2) + k, :]
                    own(ts(b, H[:, k, :], SM[:, 8 * n + k:8 * n + k + 1], None, ALU.mult))
                    stt(b[:, 1:], H[:, k, 0:T - 1], vec("rwkv_mu", 8 * n + k), b[:, 1:], ALU.mult, ALU.add)\
                        .then_inc(S("mixed"), 1)
            s0 = AT["rw_prep"][1]
            for j in range(DB):
                done(dve, m0 + 28 + j)
                for c in range(NB):
                    d = B[:, 16 + j, c * P:(c + 1) * P]
                    i = dve.tensor_tensor_scan(d, const("ones"), d, 0.0, ALU.mult, ALU.add)
                i.then_inc(S("rw_summed"), 1)
            full(dve, m0 + 43)
            for j in range(DB):
                for k in ((0, 1) if j == 0 else (j + 1,) if j + 1 < DB else ()):
                    done(dve, m0 + 8 + k)
                    ts(B[:, k, :], A[:, 8 + k, :], vec("rwkv_k_k", k), None, ALU.mult).then_inc(S("kk_raw"), 1)
                s = s0 + 2 * j
                sfull(dve, s)
                stook(ts(TM[:, j % 2, :], sbank(s)[:, :], 1e-24, None, ALU.max), s)
                done(dve, m0 + 36 + j)
                own(ts(TM[:, 2, :], B[:, 8 + j, :], -1.0, vec("rwkv_k_a", j), ALU.add, ALU.mult))
                own(stt(A[:, 8 + j, :], TM[:, 2, :], 1.0, A[:, 8 + j, :], ALU.add, ALU.mult))
                stt(TM[:, 3, :], A[:, j, :], vec("rwkv_r_k", j), A[:, 8 + j, :], ALU.mult, ALU.mult)\
                    .then_inc(S("bonus_product"), 1)
                dve.wait_ge(S("kk_root"), j + 1)
                own(dve.reciprocal(TM[:, j % 2, :], TM[:, j % 2, :]))
                own(tt(B[:, j, :], B[:, j, :], TM[:, j % 2, :], ALU.mult))
                own(tt(B[:, 8 + j, :], B[:, 8 + j, :], B[:, j, :], ALU.mult))
                s += 1
                sfull(dve, s)
                stook(tt(H[:, j, :], sbank(s)[:, :], A[:, 16 + j, :], ALU.mult), s)
            own(dve.memset(STATE, 0.0))
            def heads(x):
                return x.rearrange("p (e t) -> p e t", t=P)

            def each(m):
                return m.unsqueeze(1).to_broadcast([P, 4, P])

            def middle(i):
                c, g = STEPS[i]
                d = B[:, 16 + 2 * g:18 + 2 * g, c * P + 63:c * P + 64]
                ts(DV, d[:, :, 0], DECAY, None, ALU.mult)
                ts(DN, d[:, :, 0], -DECAY, None, ALU.mult).then_inc(S("rw_middle"), 1)

            def scale(i, part):
                c, g = STEPS[i]
                cs = slice(c * P, (c + 1) * P)
                x = scaled_of[i % 2]
                if part == 0:
                    dve.wait_ge(S("rw_decays"), i + 1)
                    stt(x[:, 0:2, :], B[:, 2 * g:2 * g + 2, cs], -1.0, GROW[:, :, 0:P], ALU.mult, ALU.mult)
                elif part == 1:
                    tt(x[:, 2:4, :], A[:, 2 * g:2 * g + 2, cs], GROW[:, :, 1:129], ALU.mult)
                    dve.tensor_copy(decay_end(c, g), GROW[:, :, 128])
                else:
                    source = B if part == 2 else A
                    tt(x[:, 2 * part:2 * part + 2, :], source[:, 8 + 2 * g:10 + 2 * g, cs], SHRINK[:, :, :], ALU.mult)\
                        .then_inc(S("rw_scaled"), 1)

            def matrix(i, j):
                s = rw_small(i, "matrix", j)
                o = 256 * (j % 2)
                sfull(dve, s)
                stook(tt(RW[:, j // 2, o:o + 256].rearrange("p (b t) -> p b t", t=P),
                         sbank(s)[:, 0:256].rearrange("p (b t) -> p b t", t=P),
                         const(MASKS[j // 2]).unsqueeze(1).to_broadcast([P, 2, P]), ALU.mult), s)

            def start_inverse(i):
                for j in range(4):
                    sdone(dve, rw_small(i, "matrix", j))
                tt(heads(INV), heads(RW[:, 0, :]), each(const("level", 0)), ALU.mult)
                own(tt(heads(INVT), heads(RW[:, 1, :]), each(const("level0_t")), ALU.mult))
                tt(heads(INV), heads(INV), each(const("ident")), ALU.add).then_inc(S("inverse_started"), 1)
                tt(heads(INVT), heads(INVT), each(const("ident")), ALU.add).then_inc(S("inverse_started"), 1)

            dve.wait_ge(S("rw_summed"), DB)
            own(dve.memset(SM[:, 70:78], 1.0))
            middle(0)
            for part in range(4):
                scale(0, part)
            for j in range(4):
                matrix(0, j)
            start_inverse(0)
            middle(1)
            for i, (c, g) in enumerate(STEPS):
                for lv in range(6):
                    s = rw_small(i, "low", lv)
                    sfull(dve, s)
                    if lv:
                        sfull(dve, rw_small(i, "invt", lv - 1))
                    stook(tt(heads(LOW), heads(sbank(s)[:, :]), each(const("level", lv + 1)), ALU.mult), s)
                    matrix(i, 4 + lv)
                    if lv == 0:
                        for half in range(2 if i else 0):
                            sdone(dve, rw_small(i - 1, "state", half))
                        dve.wait_ge(S("rw_scaled"), 2 * (i + 1))
                        for b in range(2):
                            st = ts(START[:, b, :], STATE[:, 2 * g + b, :], decay_end(c - 1, g)[:, b:b + 1],
                                    DS[i % 2][:, b:b + 1], ALU.mult, ALU.mult)
                        st.then_inc(S("rw_start"), 1)
                    elif lv <= 4 and i + 1 < len(STEPS):
                        scale(i + 1, lv - 1)
                    for what, x in (("inv", INV), ("invt", INVT))[lv == 5:]:
                        s = rw_small(i, what, lv)
                        sfull(dve, s)
                        if lv:
                            sdone(dve, rw_small(i, what, lv - 1))
                        elif what == "inv":
                            dve.wait_ge(S("inverse_started"), 2 * (i + 1))
                        stook(tt(x, x, sbank(s)[:, :], ALU.add), s)
                if i + 1 < len(STEPS):
                    for j in range(4):
                        matrix(i + 1, j)
                s = rw_small(i, "u")
                sfull(dve, s)
                stook(dve.tensor_copy(SC[:, 512:768], sbank(s)[:, 0:256]), s)
                if i + 1 < len(STEPS):
                    start_inverse(i + 1)
                if i + 2 < len(STEPS):
                    middle(i + 2)
                dve.wait_ge(S("rw_start"), i + 1)
                for half in range(2):
                    s = rw_small(i, "state", half)
                    rows = slice(64 * half, 64 * half + 64)
                    sfull(dve, s)
                    stook(tt(STATE[rows, 2 * g:2 * g + 2, :], START[rows, :, :],
                             sbank(s)[rows, 0:P].rearrange("p (b v) -> p b v", v=64), ALU.add), s)
            m0 = AT["rw_g"][0]
            for u in range(DB + 1):
                if u < DB:
                    s = gn_small("mean", u)
                    sfull(dve, s)
                    if u >= 2:
                        done(dve, m0 + u - 2)
                    stook(stt(TM[:, u % 2, :], sbank(s)[:, :], -1 / 64, A[:, u, :], ALU.mult, ALU.add), s)
                    sdone(dve, s)
                    dve.memset(SM[:, 61:62], 0.0).then_inc(S("gn_centred"), 1)
                if u == 0:
                    continue
                j = u - 1
                y, r = TM[:, j % 2, :], TM[:, 2 + j % 2, :]
                sdone(dve, gn_small("variance", j))
                own(dve.reciprocal(r, r))
                own(stt(y, y, vec("rwkv_gn_w", j), r, ALU.mult, ALU.mult))
                own(stt(y, y, vec("rwkv_gn_b", j), H[:, j, :], ALU.add, ALU.add))
                full(dve, m0 + j)
                took(tt(B[:, j, :], y, pbank(m0 + j)[:, :], ALU.mult), m0 + j)
            add_gated("rw_out", 4)
            norm2(11, 5)
            up_silu(11)
            add_gated("down11", 5)
            norm(12, lambda k: vec("final_g", k), out=S("result_ready"))


def _padded(w, rows, cols):
    out = np.zeros((rows, cols), w.dtype)
    out[:w.shape[0], :w.shape[1]] = w
    return out


def _blocks(w, by_row=False):
    k, n = -(-w.shape[0] // P), -(-w.shape[1] // P)
    b = _padded(w, k * P, n * P).reshape(k, P, n, P)
    return b.transpose((0, 2, 1, 3) if by_row else (2, 0, 1, 3)).reshape(-1, P, P)


def _gate_up(w, half):
    order = np.arange(2 * half).reshape(2, half // P, P).transpose(1, 0, 2).reshape(-1)
    return _blocks(w[:, order])


def _weights(i):
    hy, at = i["hy_w_in"][0], i["at_w_qkv"][0]
    s = [_blocks(hy[:, 0:512]), _blocks(hy[:, 1024:2048]), _blocks(hy[:, 512:1024]), _blocks(hy[:, 2560:3072]),
         _blocks(hy[:, 3072:3080]), _blocks(hy[:, 2048:2560], True), _blocks(i["hy_w_out"][0])]

    ada = np.concatenate([_blocks(i["ada_w_2"][l]) for l in range(2)]).reshape(48, 24, P, P)

    def ff(l):
        own = np.concatenate([_gate_up(i["ff_w_up"][l], 3072), _blocks(i["ff_w_down"][l])]).reshape(24, 24, P, P)
        return [np.stack([own, ada[24 * l:24 * l + 24]], axis=1).reshape(-1, P, P)]

    def ple(l):
        g, p = _blocks(i["ple_w_gate"][l]).reshape(8, 8, P, P), _blocks(i["ple_w_proj"][l]).reshape(8, 2, P, P)
        return [np.concatenate([g, p], axis=1).reshape(-1, P, P)]

    def ff2(l, j):
        return [_gate_up(i["ffn_w_in_2"][l, j], 2816), _blocks(i["ffn_w_out_2"][l, j])]

    s += ff(0) + ple(0)
    k = at[:, 1024:1280].reshape(1024, 4, 1, 64)
    s += [_blocks(at[:, 0:1024]), _blocks(np.broadcast_to(k, (1024, 4, 2, 64)).reshape(1024, 512)),
          _blocks(at[:, 1280:1536], True), _blocks(i["at_w_out"][0])]
    s += ff(1) + ple(1)
    s += ff2(0, 0)
    w = i["mla_w_in_2"][0]
    wide = np.zeros((1024, 768), w.dtype)
    wide[:, :640], wide[:, 704:736] = w[:, :640], w[:, 640:672]
    s += [_blocks(wide)]
    uq = np.zeros((384, 16, P), w.dtype)
    uq[:, :, :96] = i["mla_w_uq_2"][0].reshape(384, 16, 96)
    s += [_blocks(uq.reshape(384, 2048))]
    ukv = i["mla_w_ukv_2"][0].reshape(256, 16, 2, 64)
    s += [_blocks(np.ascontiguousarray(ukv[:, :, 0]).reshape(256, 1024))]
    uv = np.ascontiguousarray(ukv[:, :, 1]).reshape(256, 1024)
    s += [_blocks(uv[:, :512], True), _blocks(uv[:, 512:], True), _blocks(i["mla_w_out_2"][0])]
    s += ff2(0, 1) + ff2(1, 0)
    s += [_blocks(i["rwkv_w_rkv_2"][0, j]) for j in range(3)]
    s += [_blocks(i["rwkv_wd1_2"][0]), _blocks(i["rwkv_wa1_2"][0]), _blocks(i["rwkv_wg1_2"][0]),
          _blocks(i["rwkv_wd2_2"][0]), _blocks(i["rwkv_wa2_2"][0]), _blocks(i["rwkv_wg2_2"][0]),
          _blocks(i["rwkv_w_out_2"][0])]
    s += ff2(1, 1)
    blocks = np.concatenate(s)[:TILES * TILE]
    if len(blocks) < TILES * TILE:
        blocks = np.concatenate([blocks, np.zeros((TILES * TILE - len(blocks), P, P), blocks.dtype)])
    return blocks.reshape(TILES, TILE, P, P).transpose(0, 2, 1, 3).reshape(TILES, P, TILE * P)


def _vectors(i):
    def cols(a):
        return np.asarray(a, np.float32).reshape(-1, P).T

    b = i["hy_b_in"][0]
    gates = np.zeros((P, 2), np.float32)
    gates[0:4, 0], gates[0:4, 1] = b[3072:3076], b[3076:3080]
    v = {"norm_mix": cols(i["norm_mix"]), "norm_ffn": cols(i["norm_ffn"]), "norm_ple": cols(i["norm_ple"]),
         "hy_b": np.concatenate([cols(b[:3072]), gates], axis=1),
         "rg_conv_w": cols(i["rg_conv_w"]), "rg_conv_b": cols(i["rg_conv_b"]), "rg_b_a": cols(i["rg_b_a"]),
         "rg_b_x": cols(i["rg_b_x"]), "rg_lambda": cols(i["rg_lambda"]), "ml_conv_w": cols(i["ml_conv_w"]),
         "ml_conv_b": cols(i["ml_conv_b"]), "ml_norm": cols(i["ml_norm"]),
         "ff_conv_w": cols(i["ff_conv_w"]), "ff_conv_b": cols(i["ff_conv_b"]),
         "at_q_norm": cols(np.concatenate([i["at_q_norm"][0]] * 2)),
         "at_k_norm": cols(np.concatenate([i["at_k_norm"][0]] * 2)),
         "at_sinks": np.broadcast_to(i["at_sinks"][0][None, :], (P, 16)),
         "norm_g": cols(i["norm_g_2"]), "ada_b": cols(i["ada_b_2"]), "final_g": cols(i["final_g_2"]),
         "mla_q_norm": cols(i["mla_q_norm_2"]), "mla_kv_norm": cols(i["mla_kv_norm_2"]),
         "rwkv_mu": cols(i["rwkv_mu_2"]), "c": cols(i["c_2"])}
    for n in ("w0", "a0", "k_k", "k_a", "r_k", "gn_w", "gn_b"):
        v["rwkv_" + n] = cols(i[f"rwkv_{n}_2"])
    half = np.float32(10000.0) ** (-np.arange(32, dtype=np.float32) * np.float32(2.0 / 64))
    v["inv_freq"] = cols(np.tile(half, 4))
    v["eps"] = np.full((P, 1), EPS, np.float32)
    v["gn_eps"] = np.full((P, 1), 64e-5, np.float32)
    for n, k in VECTORS.items():
        assert v[n].shape == (P, k), n
    return np.concatenate([v[n] for n in VECTORS], axis=1)[:, :, None].astype(np.float32, copy=False)


def _mla_tables():
    inv = np.float32(10000.0) ** (-np.arange(0, 32, 2, dtype=np.float32) / np.float32(32))
    ang = (np.arange(T, dtype=np.float32)[None, :] * inv[:, None]).astype(np.float64)
    out = np.zeros((P, 2, T), np.float32)
    out[:, 0] = 1.0
    out[64:96, 0] = np.tile(np.cos(ang), (2, 1))
    out[64:96, 1] = np.tile(np.sin(ang), (2, 1))
    return out


def kernel(**inputs):
    import concourse.bacc as _bacc
    from concourse.bass_utils import run_bass_kernel_spmd as _run

    i = {k: np.asarray(v) for k, v in inputs.items()}
    rg = np.zeros((P, 2, 4, P), np.float32)
    for g, name in enumerate(("rg_w_a", "rg_w_x")):
        for n in range(8):
            e = 64 * (n % 2)
            rg[e:e + 64, g, n // 2, e:e + 64] = i[name][0, n]
    arrays = {
        "x": np.ascontiguousarray(i["x"][0].T),
        "p": np.ascontiguousarray(i["p"][:, 0].transpose(0, 2, 1).reshape(2, 2, P, T).transpose(0, 2, 1, 3)),
        "positions": np.ascontiguousarray(np.broadcast_to(i["positions"][0][None, :], (P, T))),
        "v_bias": np.ascontiguousarray(np.broadcast_to(i["hy_b_in"][0][None, 2048:2560], (P, T))),
        "rg_blocks": rg.reshape(P, 2, T),
        "vectors": _vectors(i),
        "constants": constants(),
        "mla_tables": _mla_tables(),
        "weights": _weights(i),
    }
    nc = _bacc.Bacc("TRN2", target_bir_lowering=False, num_devices=1)
    io = {}
    for name, a in arrays.items():
        dt = I32 if name == "positions" else F32
        io[name] = nc.dram_tensor(f"in_{name}_dram", a.shape, dt, kind="ExternalInput").ap()
    io["out"] = nc.dram_tensor("out_dram", (1024, T), F32, kind="ExternalOutput").ap()
    build(nc, io)
    r = _run(nc, [{f"in_{name}_dram": a for name, a in arrays.items()}], core_ids=[0])
    return np.ascontiguousarray(r.results[0]["out_dram"].T)[None]
```
